# Optimizing a Trainium2 kernel written in Bass

```python
import jax, jax.numpy as jnp
from jax import lax
import numpy as np

D_MODEL = 1024
BATCH = 1
SEQ = 256
DEPTH = 2

GRID_W = 64
CTX_LEN = 256
POS_BASE = 10000.0
LN_EPS = 1e-6

SSM_HEADS = 24
SSM_HEAD_DIM = 64
D_INNER = SSM_HEADS * SSM_HEAD_DIM
SSM_GROUPS = 4
HEADS_PER_GROUP = SSM_HEADS // SSM_GROUPS
SSM_STATE = 128
CONV_W = 5
CONV_CH = D_INNER + 2 * SSM_GROUPS * SSM_STATE
CHUNK = 128

FOURIER_GROUPS = 4
FOURIER_GROUP_DIM = 256
FOURIER_W = FOURIER_GROUPS * FOURIER_GROUP_DIM
N_BRANCH = 2

OFF_XBC = D_INNER
OFF_DT = OFF_XBC + CONV_CH
OFF_FOUR = OFF_DT + 2 * SSM_HEADS
OFF_GATE = OFF_FOUR + FOURIER_W
N_IN = OFF_GATE + N_BRANCH * D_MODEL

N_EXPERTS = 64
TOP_K = 8
N_EXPERT_GROUPS = 8
TOPK_GROUPS = 4
EXPERT_FF = 256
SHARED_FF = 256
ROUTE_SCALE = 2.5
MOE_BLOCK = 128

DEEPNORM_ALPHA = (2 * DEPTH) ** 0.25
DEEPNORM_BETA = (8 * DEPTH) ** -0.25

kernel_name = 'hybrid_ssd_fourier_moe_diffusion_block'

def _layer_norm(t):
    tf = t.astype(jnp.float32)
    mu = jnp.mean(tf, -1, keepdims=True)
    var = jnp.mean(jnp.square(tf - mu), -1, keepdims=True)
    return ((tf - mu) * lax.rsqrt(var + LN_EPS)).astype(t.dtype)

def _post_norm(t, g, b):
    return _layer_norm(t) * g + b

def _gated_rms_norm(y, z, w):
    h = (y * jax.nn.silu(z)).astype(jnp.float32)
    h = h * lax.rsqrt(jnp.mean(jnp.square(h), -1, keepdims=True) + LN_EPS)
    return h.astype(z.dtype) * w

def _grid_pos(rows):
    quarter = D_MODEL // 4
    omega = 1.0 / (POS_BASE ** (jnp.arange(quarter, dtype=jnp.float32) / quarter))
    ang_r = jnp.arange(rows, dtype=jnp.float32)[:, None] * omega
    ang_c = jnp.arange(GRID_W, dtype=jnp.float32)[:, None] * omega
    emb_r = jnp.concatenate([jnp.sin(ang_r), jnp.cos(ang_r)], -1)
    emb_c = jnp.concatenate([jnp.sin(ang_c), jnp.cos(ang_c)], -1)
    half = D_MODEL // 2
    emb = jnp.concatenate([jnp.broadcast_to(emb_r[:, None], (rows, GRID_W, half)),
                           jnp.broadcast_to(emb_c[None], (rows, GRID_W, half))], -1)
    return emb.reshape(rows * GRID_W, D_MODEL)

def _dwconv(t, w, b):
    out = lax.conv_general_dilated(t, w[:, None, :], window_strides=(1,),
                                   padding=[(CONV_W // 2, CONV_W // 2)],
                                   dimension_numbers=('NWC', 'WIO', 'NWC'),
                                   feature_group_count=t.shape[-1])
    return out + b

def _ssd(xh, dt, a, bm, cm, s0):
    b_, l_ = xh.shape[:2]
    nc = l_ // CHUNK
    chunk = lambda t: t.reshape((b_, nc, CHUNK) + t.shape[2:])
    adt = chunk(dt * a)
    xdt = chunk(xh.astype(jnp.float32) * dt[..., None])
    bc, cc = chunk(bm), chunk(cm)
    acum = jnp.cumsum(adt, axis=2)
    seg = acum[:, :, :, None] - acum[:, :, None, :]
    tri = jnp.tril(jnp.ones((CHUNK, CHUNK), bool))
    lmat = jnp.exp(jnp.where(tri[:, :, None, None], seg, -jnp.inf))
    scores = jnp.einsum('bclgn,bcsgn->bclsg', cc, bc)
    y_diag = jnp.einsum('bclsg,bclsgr,bcsgrp->bclgrp', scores, lmat, xdt)
    decay_states = jnp.exp(acum[:, :, -1:] - acum)
    states = jnp.einsum('bcsgn,bcsgr,bcsgrp->bcgrpn', bc, decay_states, xdt)
    chunk_decay = jnp.exp(acum[:, :, -1])

    def step(s, inp):
        dcy, st = inp
        return s * dcy[..., None, None] + st, s

    s_fin, s_prev = lax.scan(step, s0, (jnp.moveaxis(chunk_decay, 1, 0), jnp.moveaxis(states, 1, 0)))
    s_prev = jnp.moveaxis(s_prev, 0, 1)
    y_off = jnp.einsum('bclgn,bcgrpn,bclgr->bclgrp', cc, s_prev, jnp.exp(acum))
    y = (y_diag + y_off).reshape(xh.shape)
    return y.astype(xh.dtype), s_fin

def _bidir_ssd(xh, dt, a, bm, cm, s0_f, s0_b):
    y_f, s_f = _ssd(xh, dt[:, :, 0], a[0], bm, cm, s0_f)
    flip = lambda t: jnp.flip(t, axis=1)
    y_b, s_b = _ssd(flip(xh), flip(dt[:, :, 1]), a[1], flip(bm), flip(cm), s0_b)
    return y_f + flip(y_b), s_f, s_b

def _ssm_inputs(proj, conv_w, conv_b, dt_bias):
    b_, l_ = proj.shape[:2]
    z = proj[..., :OFF_XBC]
    xbc = jax.nn.silu(_dwconv(proj[..., OFF_XBC:OFF_DT], conv_w, conv_b))
    dt_raw = proj[..., OFF_DT:OFF_FOUR].reshape(b_, l_, 2, SSM_GROUPS, HEADS_PER_GROUP)
    dt = jax.nn.softplus((dt_raw + dt_bias.reshape(2, SSM_GROUPS, HEADS_PER_GROUP)).astype(jnp.float32))
    xs = xbc[..., :D_INNER].reshape(b_, l_, SSM_GROUPS, HEADS_PER_GROUP, SSM_HEAD_DIM)
    gn = SSM_GROUPS * SSM_STATE
    bm = xbc[..., D_INNER:D_INNER + gn].reshape(b_, l_, SSM_GROUPS, SSM_STATE)
    cm = xbc[..., D_INNER + gn:].reshape(b_, l_, SSM_GROUPS, SSM_STATE)
    return z, xs, dt, bm, cm

def _fourier_mix(t):
    b_, l_ = t.shape[:2]
    tg = t.reshape(b_, l_, FOURIER_GROUPS, FOURIER_GROUP_DIM).astype(jnp.float32)
    f = jnp.fft.fft2(tg, axes=(1, 3), norm='ortho').real
    return f.reshape(b_, l_, FOURIER_W).astype(t.dtype)

def _token_mixer(u, uc, w_in, conv_w, conv_b, dt_bias, a_log, d_skip, norm_w,
                 w_br_ssm, w_br_four, w_out, with_ctx):
    a = -jnp.exp(a_log.astype(jnp.float32)).reshape(2, SSM_GROUPS, HEADS_PER_GROUP)
    d = d_skip.reshape(SSM_GROUPS, HEADS_PER_GROUP, 1)
    pc = uc @ w_in
    zc, xsc, dtc, bmc, cmc = _ssm_inputs(pc, conv_w, conv_b, dt_bias)
    s0 = jnp.zeros((uc.shape[0], SSM_GROUPS, HEADS_PER_GROUP, SSM_HEAD_DIM, SSM_STATE), jnp.float32)
    yc, s_f, s_b = _bidir_ssd(xsc, dtc, a, bmc, cmc, s0, s0)
    p = u @ w_in
    z, xs, dt, bm, cm = _ssm_inputs(p, conv_w, conv_b, dt_bias)
    y, _, _ = _bidir_ssd(xs, dt, a, bm, cm, s_f, s_b)

    def merge(proj, z_, x_, y_):
        b_, l_ = proj.shape[:2]
        y_ = (y_ + x_ * d).reshape(b_, l_, D_INNER)
        ssm = _gated_rms_norm(y_, z_, norm_w) @ w_br_ssm
        four = _fourier_mix(proj[..., OFF_FOUR:OFF_GATE]) @ w_br_four
        gates = jax.nn.sigmoid(proj[..., OFF_GATE:].astype(jnp.float32)).astype(proj.dtype)
        merged = gates[..., :D_MODEL] * ssm + gates[..., D_MODEL:] * four
        return merged @ w_out

    out = merge(p, z, xs, y)
    out_c = merge(pc, zc, xsc, yc) if with_ctx else None
    return out, out_c

def _moe(h, router_w, router_bias, w1, w3, w2, ws1, ws3, ws2):
    n_tok = h.shape[0]
    scores = jax.nn.sigmoid((h @ router_w).astype(jnp.float32))
    sel = scores + router_bias.astype(jnp.float32)
    per_group = N_EXPERTS // N_EXPERT_GROUPS
    grp_score = lax.top_k(sel.reshape(n_tok, N_EXPERT_GROUPS, per_group), 2)[0].sum(-1)
    top_grp = lax.top_k(grp_score, TOPK_GROUPS)[1]
    grp_mask = jnp.any(top_grp[:, :, None] == jnp.arange(N_EXPERT_GROUPS)[None, None, :], axis=1)
    sel = jnp.where(jnp.repeat(grp_mask, per_group, axis=1), sel, -jnp.inf)
    top_e = lax.top_k(sel, TOP_K)[1]
    gate = jnp.take_along_axis(scores, top_e, axis=1)
    gate = gate / jnp.sum(gate, -1, keepdims=True) * ROUTE_SCALE
    n_asg = n_tok * TOP_K
    n_blk = -(-(n_asg + N_EXPERTS * (MOE_BLOCK - 1)) // MOE_BLOCK)
    flat_e = top_e.reshape(-1)
    flat_tok = jnp.repeat(jnp.arange(n_tok, dtype=jnp.int32), TOP_K)
    order = jnp.argsort(flat_e)
    se = flat_e[order]
    counts = jnp.bincount(flat_e, length=N_EXPERTS)
    starts = jnp.cumsum(counts) - counts
    padded = (counts + MOE_BLOCK - 1) // MOE_BLOCK * MOE_BLOCK
    pends = jnp.cumsum(padded)
    dest = (pends - padded)[se] + jnp.arange(n_asg) - starts[se]
    buf_tok = jnp.full((n_blk * MOE_BLOCK,), n_tok, jnp.int32).at[dest].set(flat_tok[order])
    buf_gate = jnp.zeros((n_blk * MOE_BLOCK,), h.dtype).at[dest].set(gate.reshape(-1)[order].astype(h.dtype))
    blk_e = jnp.minimum(jnp.searchsorted(pends, jnp.arange(n_blk) * MOE_BLOCK, side='right'), N_EXPERTS - 1)
    h_pad = jnp.concatenate([h, jnp.zeros((1, h.shape[1]), h.dtype)], 0)

    def body(acc, blk):
        tok, g, e = blk
        xb = h_pad[tok]
        hb = jax.nn.silu(xb @ w1[e]) * (xb @ w3[e])
        return acc.at[tok].add((hb @ w2[e]) * g[:, None]), None

    routed, _ = lax.scan(body, jnp.zeros_like(h_pad),
                         (buf_tok.reshape(n_blk, MOE_BLOCK), buf_gate.reshape(n_blk, MOE_BLOCK), blk_e))
    shared = (jax.nn.silu(h @ ws1) * (h @ ws3)) @ ws2
    return routed[:n_tok] + shared

def setup_inputs(seed: int = 0) -> dict:
    key = jax.random.key(seed)
    ks = jax.random.split(key, 32)
    f32 = jnp.float32
    nrm = lambda k, shape, s: jax.random.normal(k, shape, f32) * s
    dt0 = jnp.exp(jax.random.uniform(ks[8], (DEPTH, 2, SSM_HEADS), f32, np.log(1e-3), np.log(1e-1)))
    return {
        'x': nrm(ks[0], (BATCH, SEQ, D_MODEL), 1.0),
        'c': nrm(ks[1], (BATCH, D_MODEL), 1.0),
        'ctx': nrm(ks[2], (BATCH, CTX_LEN, D_MODEL), 1.0),
        'c_ctx': nrm(ks[3], (D_MODEL,), 1.0),
        'w_ada': nrm(ks[4], (DEPTH, D_MODEL, 6 * D_MODEL), 0.5 * D_MODEL ** -0.5),
        'b_ada': nrm(ks[5], (DEPTH, 6 * D_MODEL), 0.01),
        'w_in': nrm(ks[6], (DEPTH, D_MODEL, N_IN), D_MODEL ** -0.5),
        'conv_w': nrm(ks[7], (DEPTH, CONV_W, CONV_CH), CONV_W ** -0.5),
        'conv_b': nrm(ks[9], (DEPTH, CONV_CH), 0.01),
        'dt_bias': dt0 + jnp.log(-jnp.expm1(-dt0)),
        'a_log': jnp.log(jax.random.uniform(ks[10], (DEPTH, 2, SSM_HEADS), f32, 1.0, 16.0)),
        'd_skip': 1.0 + nrm(ks[11], (DEPTH, SSM_HEADS), 0.1),
        'ssm_norm_w': 1.0 + nrm(ks[12], (DEPTH, D_INNER), 0.1),
        'w_br_ssm': nrm(ks[13], (DEPTH, D_INNER, D_MODEL), DEEPNORM_BETA * D_INNER ** -0.5),
        'w_br_four': nrm(ks[14], (DEPTH, FOURIER_W, D_MODEL), DEEPNORM_BETA * FOURIER_W ** -0.5),
        'w_out': nrm(ks[15], (DEPTH, D_MODEL, D_MODEL), DEEPNORM_BETA * D_MODEL ** -0.5),
        'ln1_g': 1.0 + nrm(ks[16], (DEPTH, D_MODEL), 0.05),
        'ln1_b': nrm(ks[17], (DEPTH, D_MODEL), 0.01),
        'ln2_g': 1.0 + nrm(ks[18], (DEPTH, D_MODEL), 0.05),
        'ln2_b': nrm(ks[19], (DEPTH, D_MODEL), 0.01),
        'router_w': nrm(ks[20], (DEPTH, D_MODEL, N_EXPERTS), D_MODEL ** -0.5),
        'router_bias': nrm(ks[21], (DEPTH, N_EXPERTS), 0.01),
        'w1': nrm(ks[22], (DEPTH, N_EXPERTS, D_MODEL, EXPERT_FF), D_MODEL ** -0.5),
        'w3': nrm(ks[23], (DEPTH, N_EXPERTS, D_MODEL, EXPERT_FF), D_MODEL ** -0.5),
        'w2': nrm(ks[24], (DEPTH, N_EXPERTS, EXPERT_FF, D_MODEL), DEEPNORM_BETA * EXPERT_FF ** -0.5),
        'ws1': nrm(ks[25], (DEPTH, D_MODEL, SHARED_FF), D_MODEL ** -0.5),
        'ws3': nrm(ks[26], (DEPTH, D_MODEL, SHARED_FF), D_MODEL ** -0.5),
        'ws2': nrm(ks[27], (DEPTH, SHARED_FF, D_MODEL), DEEPNORM_BETA * SHARED_FF ** -0.5),
    }

def reference(x, c, ctx, c_ctx, w_ada, b_ada, w_in, conv_w, conv_b, dt_bias, a_log, d_skip,
              ssm_norm_w, w_br_ssm, w_br_four, w_out, ln1_g, ln1_b, ln2_g, ln2_b,
              router_w, router_bias, w1, w3, w2, ws1, ws3, ws2):
    rows = x.shape[1] // GRID_W
    x = x + _grid_pos(rows).astype(x.dtype)[None]
    xc = ctx
    silu_c = jax.nn.silu(c)
    silu_cc = jax.nn.silu(c_ctx)
    for i in range(DEPTH):
        last = i == DEPTH - 1
        mod = (silu_c @ w_ada[i] + b_ada[i])[:, None, :]
        mod_c = silu_cc @ w_ada[i] + b_ada[i]
        sh1, sc1, g1, sh2, sc2, g2 = jnp.split(mod, 6, axis=-1)
        sh1c, sc1c, g1c, sh2c, sc2c, g2c = jnp.split(mod_c, 6, axis=-1)
        u = _layer_norm(x) * (1.0 + sc1) + sh1
        uc = _layer_norm(xc) * (1.0 + sc1c) + sh1c
        f, fc = _token_mixer(u, uc, w_in[i], conv_w[i], conv_b[i], dt_bias[i], a_log[i], d_skip[i],
                             ssm_norm_w[i], w_br_ssm[i], w_br_four[i], w_out[i], not last)
        x = _post_norm(DEEPNORM_ALPHA * x + g1 * f, ln1_g[i], ln1_b[i])
        u2 = _layer_norm(x) * (1.0 + sc2) + sh2
        n_lat = u2.shape[0] * u2.shape[1]
        if last:
            m = _moe(u2.reshape(n_lat, D_MODEL), router_w[i], router_bias[i], w1[i], w3[i], w2[i],
                     ws1[i], ws3[i], ws2[i]).reshape(x.shape)
        else:
            xc = _post_norm(DEEPNORM_ALPHA * xc + g1c * fc, ln1_g[i], ln1_b[i])
            u2c = _layer_norm(xc) * (1.0 + sc2c) + sh2c
            tokens = jnp.concatenate([u2.reshape(n_lat, D_MODEL), u2c.reshape(-1, D_MODEL)], 0)
            mm = _moe(tokens, router_w[i], router_bias[i], w1[i], w3[i], w2[i], ws1[i], ws3[i], ws2[i])
            m = mm[:n_lat].reshape(x.shape)
            xc = _post_norm(DEEPNORM_ALPHA * xc + g2c * mm[n_lat:].reshape(xc.shape), ln2_g[i], ln2_b[i])
        x = _post_norm(DEEPNORM_ALPHA * x + g2 * m, ln2_g[i], ln2_b[i])
    return x


_drawn_inputs = setup_inputs


def setup_inputs(seed=0):
    import zlib

    import numpy as np

    out = dict(_drawn_inputs(seed))
    spreads = {}
    factors = {'ctx': 8.0,
     'c_ctx': 7.417,
     'b_ada': 3.682,
     'conv_b': 8.0,
     'dt_bias': 3.493,
     'a_log': 3.4,
     'd_skip': 8.0,
     'ssm_norm_w': 7.309,
     'ln1_b': 3.018,
     'ln2_b': 3.626}
    for name, (base, spread) in spreads.items():
        noise = np.random.default_rng([zlib.crc32(name.encode()), seed]).standard_normal(out[name].shape)
        drawn = base * np.exp(spread * noise) if base else spread * noise
        out[name] = __import__('jax').numpy.asarray(drawn.astype(out[name].dtype))
    for name, factor in factors.items():
        out[name] = (out[name] * factor).astype(out[name].dtype)
    return out
```

```python
import concourse.bass as bass
from concourse import mybir
import numpy as np
from contextlib import ExitStack

F32 = mybir.dt.float32
I32 = mybir.dt.int32
ACT = mybir.ActivationFunctionType
ALU = mybir.AluOpType
AX = mybir.AxisListType

P = 128
D = 1024
KD = D // P
SEQ = 256
NT = SEQ // P
DEPTH = 2
HEADS, HD, GROUPS, STATE, CONVW = 24, 64, 4, 128, 5
HPG = HEADS // GROUPS
GW = HPG * HD
DIN = HEADS * HD
CONVCH = DIN + 2 * GROUPS * STATE
OFF_XBC = DIN
OFF_DT = OFF_XBC + CONVCH
OFF_FOUR = OFF_DT + 2 * HEADS
OFF_GATE = OFF_FOUR + D
XT_TILES = DIN // P
CH_TILES = CONVCH // P
FG, FD = 4, 256
NE, FF, TOPK, NGRP, TOPG = 64, 256, 8, 8, 4
EPG = NE // NGRP
NB = 96
SENTINEL = 1 << 20
EPS = 1e-6
ALPHA = (2 * DEPTH) ** 0.25
SW = 256
NSLOT = 4
MSLOT = 3
UNR = 6

C_ID, C_LE, C_GE, C_LT, C_ONE = 0, 128, 256, 384, 512
C_P = 640
C_RANK = 641
C_TOK = C_RANK + TOPK * NE
C_TRI8 = C_TOK + TOPK
NC_COLS = C_TRI8 + NGRP * NGRP


def host_constants():
    p = np.arange(P)
    pack = np.zeros((P, NC_COLS), np.float32)
    pack[:, C_ID:C_ID + P] = np.eye(P)
    pack[:, C_LE:C_LE + P] = p[:, None] <= p[None]
    pack[:, C_GE:C_GE + P] = p[:, None] >= p[None]
    pack[:, C_LT:C_LT + P] = p[:, None] < p[None]
    pack[:, C_ONE:C_ONE + P] = 1.0
    pack[:, C_P] = p
    pack[:, C_RANK:C_RANK + TOPK * NE] = np.repeat(np.arange(TOPK), NE)[None]
    pack[:, C_TOK:C_TOK + TOPK] = p[:, None] * TOPK + np.arange(TOPK)
    g = np.arange(NGRP)
    pack[:, C_TRI8:C_TRI8 + NGRP * NGRP] = (g[None] < g[:, None]).reshape(1, -1)
    n = np.arange(SEQ)
    ang = 2 * np.pi * ((n[:, None] * n[None]) % SEQ) / SEQ
    dft = np.zeros((2, SEQ, 2 * SEQ), np.float32)
    dft[0] = np.concatenate([np.cos(ang), np.sin(ang)], 1)
    dft[1] = np.concatenate([np.cos(ang), -np.sin(ang)], 1) / SEQ
    quarter = D // 4
    omega = (np.float32(1.0) / (np.float32(10000.0) ** (np.arange(quarter, dtype=np.float32) / np.float32(quarter)))).astype(np.float32)
    grid_w = 64
    rows = SEQ // grid_w
    def emb(k):
        a = (np.arange(k, dtype=np.float32)[:, None] * omega).astype(np.float32)
        return np.concatenate([np.sin(a), np.cos(a)], -1)
    er, ec = emb(rows), emb(grid_w)
    pos = np.concatenate([np.broadcast_to(er[:, None], (rows, grid_w, D // 2)),
                          np.broadcast_to(ec[None], (rows, grid_w, D // 2))], -1)
    return pack, dft, np.ascontiguousarray(pos.reshape(SEQ, D).astype(np.float32))


CALLS = [(0, 1, True), (0, 0, True), (1, 1, False), (1, 0, True)]
TILES = {0: [0, 1], 1: [2, 3]}
MOE_TILES = {0: [0, 1, 2, 3], 1: [0, 1]}


def slabs_of(full):
    out = []
    if full:
        out += [("four", j) for j in range(4)]
    out += [("dt", 0)]
    out += [("xbc", j) for j in range(10 if full else 8)]
    if full:
        out += [("z", j) for j in range(6)]
        for j in range(4):
            out += [("g2", j), ("bf", j)]
        out += [("g1", j) for j in range(4)]
        for j in range(4):
            out += [("bsa", j), ("bsb", j)]
        out += [("wo", j) for j in range(4)]
    return out


SLABS = [(m, kind, j) for m, (_, _, full) in enumerate(CALLS) for kind, j in slabs_of(full)]
SLAB_NO = {s: n for n, s in enumerate(SLABS)}
BANK_NO, READER = {}, []
for s in SLABS:
    if s[1] == "bsb":
        BANK_NO[s] = BANK_NO[(s[0], "bsa", s[2])]
    else:
        BANK_NO[s] = len(READER)
        READER.append("act" if s[1] in ("four", "z", "g1", "g2") else "dve")


def freed(bank_no):
    who = READER[bank_no]
    return who, sum(r == who for r in READER[:bank_no + 1])


class Stage:
    def __init__(self, sem, counts):
        self.sem, self.counts = sem, counts

    def at(self, m, k):
        assert 0 < k <= self.counts[m]
        return sum(self.counts[:m]) + k

    def all(self, m):
        return sum(self.counts[:m + 1])


def hybrid_block_kernel(nc, ins, consts, dfts, grid, out, scratch, dbg=None):
    ctx = ExitStack()
    with ctx:
        def sb(name, shape, dt=F32):
            return ctx.enter_context(nc.sbuf_tensor(name, shape, dt))

        def sem(name):
            return ctx.enter_context(nc.semaphore(name))

        def stage(name, full, part=0):
            return Stage(sem(name), [full if f else part for _, _, f in CALLS])

        xres = sb("xres", [P, 4, D])
        cst = sb("cst", [P, NC_COLS])
        ident, tri_le, tri_ge, tri_lt, ones = (cst[:, o:o + P] for o in (C_ID, C_LE, C_GE, C_LT, C_ONE))
        dft = sb("dft", [P, 2, NT, 2 * SEQ])
        modc = sb("modc", [P, 48, 2])
        csil = sb("csil", [P, KD, 2])
        craw = sb("craw", [P, 2, KD])
        lnrow = sb("lnrow", [P, 2, D])
        grow = sb("grow", [P, 2, D])
        par = sb("par", [P, 180])
        praw = sb("praw", [120, 2, P])
        hpar = sb("hpar", [P, 120])
        aneg = sb("aneg", [P, 48])
        stat = sb("stat", [P, 2, 6])
        mv = sb("mv", [P, 2])
        rstd = sb("rstd", [P, 2])
        epsc = sb("epsc", [P, 1])
        modrow = sb("modrow", [2, 2, SW])
        arena = sb("arena", [P, 39600])
        used = [0]

        def carve(n, at=None):
            o = used[0] if at is None else at
            if at is None:
                used[0] += n
            assert o + n <= 39600, (o, n)
            return arena[:, o:o + n]

        ring = [carve(KD * SW).rearrange("p (k n) -> p k n", n=SW) for _ in range(NSLOT)]
        uT = carve(KD * SEQ).rearrange("p (k t) -> p k t", k=KD)
        mT = carve(KD * SEQ).rearrange("p (k t) -> p k t", k=KD)
        xs_at = used[0]
        xs = carve(NT * DIN).rearrange("p (c n) -> p c n", c=NT)
        ynT = carve(XT_TILES * SEQ, xs_at).rearrange("p (k t) -> p k t", k=XT_TILES)
        zs = carve(NT * DIN).rearrange("p (c n) -> p c n", c=NT)
        btok = carve(NT * GROUPS * STATE).rearrange("p (c n) -> p c n", c=NT)
        bT = carve(GROUPS * SEQ).rearrange("p (g t) -> p g t", g=GROUPS)
        cT = carve(GROUPS * SEQ).rearrange("p (g t) -> p g t", g=GROUPS)
        st = [[carve(DIN).rearrange("p (h d) -> p h d", h=HEADS) for _ in range(2)] for _ in range(2)]
        seg_at = used[0]
        seg = carve(2 * HPG * P).rearrange("p (d h l) -> p d h l", d=2, h=HPG)
        smask = carve(2 * P).rearrange("p (d l) -> p d l", d=2)
        ytmp = carve(3 * GW).rearrange("p (b n) -> p b n", b=3)
        fA = carve(2 * NT * 2 * FD, seg_at).rearrange("p (b t n) -> p b t n", b=2, t=NT)
        lnx_at = used[0]
        xdt = carve(2 * 2 * GW).rearrange("p (b d n) -> p b d n", b=2, d=2)
        wst = carve(2 * GW).rearrange("p (b n) -> p b n", b=2)
        lnx = carve(2 * D, lnx_at).rearrange("p (b n) -> p b n", b=2)
        cacc = grow[:, 1, :].rearrange("p (b t) -> p b t", b=4)
        cxt = carve(4 * SEQ).rearrange("p (b t) -> p b t", b=4)
        fT = carve(KD * SEQ).rearrange("p (k t) -> p k t", k=KD)
        fO = carve(KD * SEQ).rearrange("p (k t) -> p k t", k=KD)
        gT = fT
        dtv = carve(NT * 48).rearrange("p (c n) -> p c n", c=NT)
        adt = carve(NT * 48).rearrange("p (c n) -> p c n", c=NT)
        acu = carve(NT * 96).rearrange("p (c n) -> p c n", c=NT)
        eac = carve(NT * 48).rearrange("p (c n) -> p c n", c=NT)
        dec = carve(NT * 48).rearrange("p (c n) -> p c n", c=NT)
        ecd = carve(NT * 48).rearrange("p (c n) -> p c n", c=NT)
        sp = [carve(NT * 48).rearrange("p (c n) -> p c n", c=NT) for _ in range(4)]
        yrow = cxt[:, 0:2, :]
        rss = carve(NT * 2).rearrange("p (c n) -> p c n", c=NT)
        mixer_words = used[0]

        used[0] = 0
        ew = [carve(6 * D) for _ in range(MSLOT)]
        w13 = [w[:, 0:4 * D].rearrange("p (k n) -> p k n", k=KD) for w in ew]
        w2s = [w[:, 4 * D:6 * D].rearrange("p (k n) -> p k n", k=2) for w in ew]
        yall = arena[:, 0:TOPK * D].rearrange("p (j n) -> p j n", j=TOPK)
        u2T = carve(KD * 4 * P).rearrange("p (k t) -> p k t", k=KD)
        macc = carve(4 * D).rearrange("p (t n) -> p t n", t=4)
        xg = [carve(D) for _ in range(3)]
        xTe = [carve(D).rearrange("p (k t) -> p k t", k=KD) for _ in range(2)]
        hs = [carve(FF) for _ in range(2)]
        hh = [carve(FF) for _ in range(2)]
        hT = [carve(2 * P).rearrange("p (k t) -> p k t", k=2) for _ in range(2)]
        ysb = [carve(D) for _ in range(2)]
        ln2x = carve(2 * D).rearrange("p (b n) -> p b n", b=2)
        rw = carve(KD * NE).rearrange("p (k e) -> p k e", k=KD)
        rbias = carve(NE)
        msk = carve(4 * NE).rearrange("p (t e) -> p t e", t=4)
        gat = carve(4 * TOPK).rearrange("p (t j) -> p t j", t=4)
        rt = [carve(NE) for _ in range(8)]
        r8 = [carve(8) for _ in range(6)]
        cube = carve(TOPK * NE)
        slotf = carve(4 * TOPK).rearrange("p (t j) -> p t j", t=4)
        print("words", mixer_words, used[0])
        sloti = sb("sloti", [P, 4, TOPK], I32)
        tokid = sb("tokid", [P, 4, TOPK], I32)
        tbl = sb("tbl", [P, NB + UNR], I32)
        tblg = sb("tblg", [P, NB + UNR], I32)
        idg = sb("idg", [P, UNR], I32)
        ids = sb("ids", [P, UNR], I32)
        sent = sb("sent", [P, NB], I32)
        bexp = sb("bexp", [1, P + 2], I32)
        ecol = sb("ecol", [P, 1])
        first = sb("first", [P, 2], I32)

        psum = ctx.enter_context(nc.psum_tensor("psum", [P, 8, 512], F32))
        bank = [psum[:, i, :] for i in range(8)]

        s_const = sem("constants_in")
        s_x = sem("x_in")
        s_pos = sem("pos_in")
        s_c = sem("c_in")
        s_csil = sem("csil_ready")
        s_xin = sem("x_plus_pos")
        s_par = sem("params_in")
        s_tp_par = sem("params_transposed")
        s_parc = sem("params_ready")
        s_lnrow = sem("lnrow_in")
        s_lnrow_free = sem("lnrow_used")
        s_ada = [sem(f"ada_in{i}") for i in range(4)]
        s_ada_mm = sem("ada_product")
        s_ada_row = sem("ada_row")
        s_ada_tp = sem("ada_transposed")
        s_ada_col = sem("ada_col")
        s_modc = sem("modulation_ready")
        s_slab_in = [sem(f"slab_in{i}") for i in range(NSLOT)]
        s_slab = sem("slab_product")
        s_read = {"act": sem("act_read_product"), "dve": sem("dve_read_product")}
        s_var = sem("ln_variance")
        s_std = sem("ln_std")
        s_chain = sem("dve_chain")
        s_achain = sem("act_chain")
        s_pchain = sem("pool_chain")
        t_lnx = stage("u_normed", 2, 2)
        t_utp = stage("u_transposed", 2, 2)
        t_uT = stage("u_ready", 2, 2)
        t_acc = stage("conv_first_tap", 10, 8)
        t_cv = stage("conv_done", 10, 8)
        t_cs = stage("conv_silu", 10, 8)
        t_ctp = stage("conv_transposed", 8, 8)
        t_xs = stage("conv_token_major", 8, 8)
        t_dtx = stage("dt_exp", 1, 1)
        t_dtr = stage("dt_raw", 1, 1)
        t_adt = stage("adt_ready", 1, 1)
        t_acp = stage("cumulated_product", 1, 1)
        t_acu = stage("cumulated_ready", 1, 1)
        t_eac = stage("exp_cumulated", 1, 1)
        t_dec = stage("decay_ready", 1, 1)
        t_w = Stage(sem("weighted_x_ready"), [16 if c[1] else 8 for c in CALLS])
        t_stp = Stage(sem("state_product"), [16 if c[1] else 8 for c in CALLS])
        t_st = Stage(sem("state_ready"), [16 if c[1] else 8 for c in CALLS])
        t_f1 = stage("dft_feature_product", 4, 0)
        t_f1c = stage("dft_feature_ready", 4, 0)
        t_f2 = stage("dft_token_product", 4, 0)
        t_f2c = stage("dft_token_ready", 4, 0)
        t_row = stage("cumulated_rows", 16, 0)
        t_rowr = stage("cumulated_rows_read", 16, 0)
        t_seg = stage("segments_ready", 8, 0)
        t_exp = stage("decay_matrix", 8, 0)
        t_sm = stage("masked_scores", 8, 0)
        t_lmF = stage("weighted_scores_forward", 8, 0)
        t_lmB = stage("weighted_scores_backward", 8, 0)
        t_xd = stage("x_dt_ready", 8, 0)
        t_y = stage("y_products", 8, 0)
        t_yr = stage("y_products_read", 8, 0)
        t_h = stage("gated_y", 2, 0)
        t_ss = stage("square_sum", 2, 0)
        t_yn = stage("normed_y", 2, 0)
        t_ytp = stage("y_transposed", 6, 0)
        t_yT = stage("y_channel_major", 6, 0)
        t_mT2 = stage("fourier_merged", 4, 0)
        t_mT = stage("merged", 4, 0)
        t_gd = stage("gate_diagonals", 8, 0)
        t_gp = stage("gate_rows_product", 1, 0)
        t_gr = stage("gate_rows_ready", 1, 0)

        names = ("u2_normed u2_transposed u2_ready logits routed counted placed rank_tp blocks_ready "
                 "back_tp back_copied u2_stored sentinel_in table_scattered table_in table_ready "
                 "router_in shared_in shared_up shared_sil shared_h shared_ht shared_htc shared_y shared_out "
                 "g2_diag g2_rows g2_ready scores").split()
        s = {n: sem(n) for n in names}
        nt0 = len(MOE_TILES[0])
        fixed = {"counted": 1, "placed": 1, "rank_tp": 1, "blocks_ready": 1, "u2_stored": 16 * nt0, "sentinel_in": 16,
                 "table_scattered": 16 * nt0 * TOPK, "table_in": 16, "router_in": 32, "shared_in": 48,
                 "g2_diag": KD * nt0 // 2, "g2_rows": nt0 // 2, "g2_ready": nt0 // 2}

        def of(l, name, k):
            return k + (fixed.get(name, nt0) if l else 0)

        e_names = "xt_tp xt_act xt_dve up silu h_ready ht_tp ht_copied down y_act y_dve".split()
        e = [{n: sem(f"e_{n}{l}") for n in e_names} for l in range(DEPTH)]
        e_w = [[sem(f"e_w{l}{i}") for i in range(MSLOT)] for l in range(DEPTH)]
        e_g = [[sem(f"e_g{l}{i}") for i in range(3)] for l in range(DEPTH)]
        e_s = [[sem(f"e_s{l}{i}") for i in range(2)] for l in range(DEPTH)]
        e_yin = [sem(f"e_yin{l}") for l in range(DEPTH)]
        e_comb = [sem(f"e_comb{l}") for l in range(DEPTH)]
        s_shift = [sem(f"token_table{l}") for l in range(DEPTH)]
        s_idg = [sem(f"gather_index{l}") for l in range(DEPTH)]
        s_ids = [sem(f"scatter_index{l}") for l in range(DEPTH)]
        s_passed = sem("pool_passed")
        s_out = sem("out_stored")

        block = ctx.enter_context(nc.Block())

        def ada_cols(i):
            return bass.ds(i * SW, SW)

        @block.sync
        def _(sp):
            sp.dma_start(cst[:, :], consts).then_inc(s_const, 16)
            sp.dma_start(craw[:, 0, :], ins["c"][0].rearrange("(p k) -> p k", k=KD)).then_inc(s_c, 16)
            sp.dma_start(craw[:, 1, :], ins["c_ctx"].rearrange("(p k) -> p k", k=KD)).then_inc(s_c, 16)
            for t in range(NT):
                sp.dma_start(xres[:, t, :], ins["x"][0, t * P:(t + 1) * P, :]).then_inc(s_x, 16)
                sp.dma_start(xres[:, NT + t, :], ins["ctx"][0, t * P:(t + 1) * P, :]).then_inc(s_x, 16)
                sp.dma_start(lnx[:, t, :], grid[t * P:(t + 1) * P, :]).then_inc(s_pos, 16)
            for a in range(2):
                sp.dma_start(dft[:, a, :, :], dfts[a].rearrange("(t p) n -> p t n", p=P)).then_inc(s_const, 16)

            def params(l):
                if l:
                    sp.wait_ge(s_parc, 2 * l)
                    sp.wait_ge(t_yT.sem, t_yT.all(1))
                    sp.wait_ge(t_yn.sem, t_yn.all(1))
                sp.dma_start(praw[0:48, 0, :], ins["b_ada"][l].rearrange("(j p) -> j p", p=P)).then_inc(s_par, 16)
                sp.dma_start(praw[48:60, 0, :], ins["ssm_norm_w"][l].rearrange("(j p) -> j p", p=P)).then_inc(s_par, 16)
                sp.dma_start(praw[0:100, 1, :], ins["conv_w"][l].rearrange("t (j p) -> (t j) p", p=P)).then_inc(s_par, 16)
                sp.dma_start(praw[100:120, 1, :], ins["conv_b"][l].rearrange("(j p) -> j p", p=P)).then_inc(s_par, 16)
                hp = [(0, 48, ins["dt_bias"][l:l + 1].rearrange("a d h -> a (d h)")),
                      (48, 48, ins["a_log"][l:l + 1].rearrange("a d h -> a (d h)")),
                      (96, 24, ins["d_skip"][l:l + 1, :])]
                for o, n, src in hp:
                    sp.dma_start(hpar[:, o:o + n], src.to_broadcast([P, n])).then_inc(s_par, 16)

            def modulation(l):
                wsrc = ins["w_ada"][l].rearrange("(p k) n -> p k n", k=KD)
                with sp.Fori(0, 6) as i:
                    for b in range(4):
                        sp.wait_ge(s_ada_mm, (i * 4 + b + 1) + 28 * l)
                        sp.dma_start(ring[b][:, :, :], wsrc[:, :, ada_cols(i * 4 + b)]).then_inc(s_ada[b], 16)

            def slab(m, kind, j):
                l = CALLS[m][0]
                n = SLAB_NO[(m, kind, j)]
                if n >= NSLOT:
                    sp.wait_ge(s_slab, n - NSLOT + 1)
                slot, w = ring[n % NSLOT], ins["w_in"][l]
                if kind in ("bsa", "bsb"):
                    k0 = 6 if kind == "bsb" else 0
                    src = ins["w_br_ssm"][l].rearrange("(k p) n -> p k n", p=P)[:, k0:k0 + 6, j * SW:(j + 1) * SW]
                    sp.dma_start(slot[:, 0:6, :], src).then_inc(s_slab_in[n % NSLOT], 16)
                    return
                c0, cn = {"four": (OFF_FOUR, SW), "xbc": (OFF_XBC, SW), "z": (0, SW), "dt": (OFF_DT, 48),
                          "g1": (OFF_GATE, SW), "g2": (OFF_GATE + D, SW)}.get(kind, (0, SW))
                if kind == "bf":
                    w = ins["w_br_four"][l]
                if kind == "wo":
                    w = ins["w_out"][l]
                src = w.rearrange("(k p) n -> p k n", p=P)[:, :, c0 + j * cn:c0 + (j + 1) * cn]
                sp.dma_start(slot[:, :, 0:cn], src).then_inc(s_slab_in[n % NSLOT], 16)

            def post_norm_rows(l, g, b, which):
                if which:
                    sp.wait_ge(s_lnrow_free, which)
                sp.dma_start(lnrow[:, 0, :], ins[g][l:l + 1, :].to_broadcast([P, D])).then_inc(s_lnrow, 16)
                sp.dma_start(lnrow[:, 1, :], ins[b][l:l + 1, :].to_broadcast([P, D])).then_inc(s_lnrow, 16)

            norm = 0
            for l in range(DEPTH):
                params(l)
                if l:
                    sp.wait_ge(e_comb[l - 1], len(MOE_TILES[l - 1]))
                modulation(l)
                sp.wait_ge(s_ada_mm, 24 * (l + 1) + 4 * (l + 1))
                for m, (cl, _, full) in enumerate(CALLS):
                    if cl == l:
                        if full:
                            post_norm_rows(l, "ln1_g", "ln1_b", norm)
                            norm += 1
                        for kind, j in slabs_of(full):
                            slab(m, kind, j)
                nt = len(MOE_TILES[l])
                m = 2 * l + 1
                sp.wait_ge(t_mT.sem, t_mT.all(m))
                sp.wait_ge(s_slab, SLAB_NO[(m, "wo", 3)] + 1)
                sp.wait_ge(s_lnrow_free, norm)
                sp.dma_start(rw[:, :, :], ins["router_w"][l].rearrange("(k p) n -> p k n", p=P)).then_inc(s["router_in"], 16)
                sp.dma_start(rbias[:, :], ins["router_bias"][l:l + 1, :].to_broadcast([P, NE])).then_inc(s["router_in"], 16)
                sp.dma_start(w13[2][:, :, 0:FF], ins["ws1"][l].rearrange("(k p) n -> p k n", p=P)).then_inc(s["shared_in"], 16)
                sp.dma_start(w13[2][:, :, FF:2 * FF], ins["ws3"][l].rearrange("(k p) n -> p k n", p=P)).then_inc(s["shared_in"], 16)
                sp.dma_start(w2s[2][:, :, :], ins["ws2"][l].rearrange("(k p) n -> p k n", p=P)).then_inc(s["shared_in"], 16)
                post_norm_rows(l, "ln2_g", "ln2_b", norm)
                norm += 1
                for i, t in enumerate(MOE_TILES[l]):
                    sp.wait_ge(s["back_copied"], of(l, "back_copied", i + 1))
                    sp.dma_start(scratch["u2"][l][i * P:(i + 1) * P, :], macc[:, i, :]).then_inc(s["u2_stored"], 16)
                sp.wait_ge(s["blocks_ready"], of(l, "blocks_ready", 1))
                n = sp.value_load(bexp[0:1, P:P + 1], min_val=1, max_val=NB)

                def expert_in(i, b):
                    ex = sp.value_load(bexp[0:1, bass.ds(i, 1)], min_val=0, max_val=NE - 1)
                    sp.wait_ge(e[l]["down"], i + 1)
                    for dst, src in ((w13[b][:, :, 0:FF], "w1"), (w13[b][:, :, FF:2 * FF], "w3")):
                        sp.dma_start(dst, ins[src][l, bass.ds(ex, 1), :, :].rearrange("a (k p) n -> p (a k) n", p=P)).then_inc(e_w[l][b], 16)
                    sp.dma_start(w2s[b][:, :, :], ins["w2"][l, bass.ds(ex, 1), :, :].rearrange("a (k p) n -> p (a k) n", p=P)).then_inc(e_w[l][b], 16)

                expert_in(0, 0)
                expert_in(1, 1)
                sp.wait_ge(s["shared_y"], of(l, "shared_y", nt))
                with sp.Fori(0, NB // UNR) as ii:
                    for u in range(UNR):
                        i = ii * UNR + (u + 2)
                        with sp.If(n > i):
                            expert_in(i, (u + 2) % MSLOT)
                stored = [sp.snap(((n + 1) // 2 + 1) * 16), sp.snap((n // 2 + 1) * 16)]
                sp.wait_ge(e_s[l][0], stored[0])
                sp.wait_ge(e_s[l][1], stored[1])
                for i in range(nt):
                    if i:
                        sp.wait_ge(e_comb[l], i)
                    sp.dma_start(yall[:, :, :], scratch["y"][l][i * P * TOPK:(i + 1) * P * TOPK, :].rearrange("(p j) n -> p j n", j=TOPK)).then_inc(e_yin[l], 16)
            for i in range(NT):
                sp.wait_ge(e_comb[1], i + 1)
                sp.dma_start(out[0, i * P:(i + 1) * P, :], xres[:, i, :]).then_inc(s_out, 16)
            sp.wait_ge(s_out, 16 * NT)

        @block.tensor
        def _(pe):
            mm = nc.tensor.matmul
            tp = nc.tensor.transpose
            pe.sem_inc(s_ada_mm, 4)
            pe.wait_ge(s_const, 48)
            for l in range(DEPTH):
                pe.wait_ge(s_par, 16 * 7 * (l + 1))
                if l:
                    pe.wait_ge(e_comb[l - 1], len(MOE_TILES[l - 1]))
                tp(bank[7][:, 0:60], praw[0:60, 0, :], ident[0:60, 0:60])
                tp(bank[7][:, 60:180], praw[0:120, 1, :], ident[0:120, 0:120]).then_inc(s_tp_par, 1)
                pe.wait_ge(s_csil, 1)
                with pe.Fori(0, 6) as i:
                    for b in range(4):
                        pe.wait_ge(s_ada_row, i * 4 + b + 1 + 24 * l)
                        pe.wait_ge(s_ada[b], (i + 1) * 16 + 96 * l)
                        for k in range(KD):
                            last = mm(bank[b % 2][0:2, 0:SW], csil[:, k, :], ring[b][:, k, :], start=k == 0, stop=k == KD - 1)
                        last.then_inc(s_ada_mm, 1)
                        pe.wait_ge(s_ada_row, i * 4 + b + 3 + 24 * l)
                        pe.wait_ge(s_ada_col, i * 4 + b + 1 + 24 * l)
                        mm(bank[3][:, 0:2], modrow[:, b % 2, 0:P], ident[0:2, 0:2], start=True, stop=True)
                        mm(bank[3][:, 2:4], modrow[:, b % 2, P:2 * P], ident[0:2, 0:2], start=True, stop=True).then_inc(s_ada_tp, 1)
                pe.sem_inc(s_ada_mm, 4)

                for m, (cl, stream, full) in enumerate(CALLS):
                    if cl != l:
                        continue
                    for t in range(NT):
                        pe.wait_ge(t_lnx.sem, t_lnx.at(m, t + 1))
                        if t == 0:
                            pe.wait_ge(s_modc, l + 1)
                        for k in range(KD):
                            last = tp(psum[:, 3 + 2 * t + k // 4, (k % 4) * P:(k % 4 + 1) * P], lnx[:, t, k * P:(k + 1) * P], ident)
                        last.then_inc(t_utp.sem, 1)
                    pe.wait_ge(t_uT.sem, t_uT.at(m, 2))

                    def begin(kind, j):
                        n = SLAB_NO[(m, kind, j)]
                        b = BANK_NO[(m, kind, j)]
                        pe.wait_ge(s_slab_in[n % NSLOT], 16 * (n // NSLOT + 1))
                        if b >= 2 and kind != "bsb":
                            who, cnt = freed(b - 2)
                            pe.wait_ge(s_read[who], cnt)
                        return ring[n % NSLOT], bank[b % 2].rearrange("p (a t) -> p a t", a=2)

                    def channel_major(kind, j, rhs, ks, first=True, final=True):
                        w, o = begin(kind, j)
                        for a in range(2):
                            for k in range(ks):
                                last = mm(o[:, a, :], w[:, k, a * P:(a + 1) * P], rhs[:, k, :],
                                          start=first and k == 0, stop=final and k == ks - 1, skip_group_check=True)
                        last.then_inc(s_slab, 1)

                    def token_major(kind, j, lhs, cols):
                        w, o = begin(kind, j)
                        for a in range(NT):
                            for k in range(KD):
                                last = mm(o[:, a, 0:cols], lhs[:, k, a * P:(a + 1) * P], w[:, k, 0:cols], start=k == 0, stop=k == KD - 1)
                        last.then_inc(s_slab, 1)

                    def conv_transpose(j):
                        pe.wait_ge(t_cs.sem, t_cs.at(m, j + 1))
                        if j >= 2:
                            pe.wait_ge(t_xs.sem, t_xs.at(m, j - 1))
                        o = bank[2 + 5 * (j % 2)]
                        for a in range(2):
                            ch = 2 * j + a
                            src = cxt[:, (2 * j + a) % 4, :] if ch < XT_TILES else bT[:, ch - XT_TILES, :]
                            for c in range(NT):
                                last = tp(o[:, c * SW + a * P:c * SW + (a + 1) * P], src[:, c * P:(c + 1) * P], ident)
                        last.then_inc(t_ctp.sem, 1)

                    if full:
                        for j in range(4):
                            channel_major("four", j, uT, KD)
                    token_major("dt", 0, uT, 48)
                    for j in range(10 if full else 8):
                        channel_major("xbc", j, uT, KD)
                        if 2 <= j < 10:
                            conv_transpose(j - 2)
                    if not full:
                        conv_transpose(6)
                        conv_transpose(7)
                    pe.wait_ge(t_adt.sem, t_adt.at(m, 1))
                    for c in range(NT):
                        mm(bank[5][:, c * 96:c * 96 + 24], tri_le, adt[:, c, 0:24], start=True, stop=True)
                        mm(bank[5][:, c * 96 + 24:c * 96 + 48], tri_ge, adt[:, c, 24:48], start=True, stop=True)
                        last = mm(bank[5][:, c * 96 + 48:c * 96 + 96], ones, adt[:, c, :], start=True, stop=True)
                    last.then_inc(t_acp.sem, 1)
                    if full:
                        for j in range(6):
                            token_major("z", j, uT, SW)

                        def feature_dft(g):
                            if g >= 1:
                                pe.wait_ge(t_f1c.sem, t_f1c.at(m, g))
                            for t in range(NT):
                                for k in range(2):
                                    last = mm(bank[3 + t][:, :], fT[:, 2 * g + k, t * P:(t + 1) * P], dft[:, 0, k, :], start=k == 0, stop=k == 1)
                            last.then_inc(t_f1.sem, 1)

                        def token_dft(g):
                            pe.wait_ge(t_f1c.sem, t_f1c.at(m, g + 1))
                            if g >= 1:
                                pe.wait_ge(t_f2c.sem, t_f2c.at(m, g))
                            for a in range(2):
                                for i, (t, part) in enumerate([(t, part) for t in range(NT) for part in range(2)]):
                                    last = mm(bank[6][:, a * SEQ:(a + 1) * SEQ],
                                              fA[:, g % 2, t, part * FD + a * P:part * FD + (a + 1) * P],
                                              dft[:, 1, t, part * SEQ:(part + 1) * SEQ], start=i == 0, stop=i == 3)
                            last.then_inc(t_f2.sem, 1)

                        for g in range(GROUPS):
                            feature_dft(g)
                            if g:
                                token_dft(g - 1)
                        token_dft(GROUPS - 1)

                    def state_product(i, c, g):
                        pe.wait_ge(t_w.sem, t_w.at(m, i + 1))
                        if i == 0:
                            pe.wait_ge(t_acu.sem, t_acu.at(m, 1))
                        if i == 0 and full:
                            pe.wait_ge(t_f2c.sem, t_f2c.at(m, 4))
                        if i >= 2:
                            pe.wait_ge(t_st.sem, t_st.at(m, i - 1))
                        mm(bank[5 + i % 2][:, 0:GW], btok[:, c, g * STATE:(g + 1) * STATE], wst[:, i % 2, :], start=True, stop=True).then_inc(t_stp.sem, 1)

                    pe.wait_ge(t_xs.sem, t_xs.at(m, 8))
                    for i, (c, g) in enumerate([(0, g) for g in range(4)] + [(1, g) for g in range(4)]):
                        state_product(i, c, g)

                    if full:
                        def rows(it):
                            c, g = it // GROUPS, it % GROUPS
                            for d in range(2):
                                if it or d:
                                    pe.wait_ge(t_rowr.sem, t_rowr.at(m, 2 * it + d))
                                if d == 0:
                                    mm(bank[4][:, 256:384], bT[:, g, c * P:(c + 1) * P], cT[:, g, c * P:(c + 1) * P], start=True, stop=True)
                                tri = tri_le if d == 0 else tri_ge
                                for r in range(HPG):
                                    h = d * HEADS + g * HPG + r
                                    last = mm(psum[:, 3 + r // 4, (r % 4) * P:(r % 4 + 1) * P],
                                              adt[:, c, h:h + 1].to_broadcast([P, P]), tri, start=True, stop=True)
                                last.then_inc(t_row.sem, 1)

                        def y_products(it):
                            c, g = it // GROUPS, it % GROUPS
                            pe.wait_ge(t_lmF.sem, t_lmF.at(m, it + 1))
                            pe.wait_ge(t_lmB.sem, t_lmB.at(m, it + 1))
                            pe.wait_ge(t_xd.sem, t_xd.at(m, it + 1))
                            if it:
                                pe.wait_ge(t_yr.sem, t_yr.at(m, it))
                            else:
                                pe.wait_ge(t_st.sem, t_st.at(m, 8))
                            for r in range(HPG):
                                o = bank[5][:, r * HD:(r + 1) * HD]
                                mm(o, seg[:, 0, r, :], xdt[:, it % 2, 0, r * HD:(r + 1) * HD], start=True, stop=False)
                                last = mm(o, seg[:, 1, r, :], xdt[:, it % 2, 1, r * HD:(r + 1) * HD], start=False, stop=True)
                            for d in range(2):
                                which = c if d == 0 else 1 - c
                                if stream == 0 or which == 1:
                                    last = mm(bank[6 + d][:, 0:GW], cT[:, g, c * P:(c + 1) * P],
                                              st[d][which][:, g * HPG:(g + 1) * HPG, :].rearrange("p h d -> p (h d)"), start=True, stop=True)
                            last.then_inc(t_y.sem, 1)

                        for it in range(8):
                            if it == 0:
                                pe.wait_ge(t_cs.sem, t_cs.at(m, 10))
                                pe.wait_ge(t_xs.sem, t_xs.at(m, 8))
                            rows(it)
                            j = it // 2
                            channel_major("g2" if it % 2 == 0 else "bf", j, uT if it % 2 == 0 else fO, KD)
                            y_products(it)

                    if stream == 1:
                        for i, (c, g) in enumerate([(1, g) for g in range(4)] + [(0, g) for g in range(4)]):
                            state_product(8 + i, c, g)

                    if full:
                        for j in range(4):
                            channel_major("g1", j, uT, KD)
                        for c in range(NT):
                            pe.wait_ge(t_yn.sem, t_yn.at(m, c + 1))
                            for b in range(3):
                                k = 3 * c + b
                                if k >= 2:
                                    pe.wait_ge(t_yT.sem, t_yT.at(m, k - 1))
                                for a in range(4):
                                    ch = 4 * b + a
                                    last = tp(bank[2 + 5 * (k % 2)][:, a * P:(a + 1) * P], zs[:, c, ch * P:(ch + 1) * P], ident)
                                last.then_inc(t_ytp.sem, 1)
                        pe.wait_ge(t_yT.sem, t_yT.at(m, 6))
                        for j in range(4):
                            w, o = begin("bsa", j)
                            w2, _ = begin("bsb", j)
                            for a in range(2):
                                for k in range(6):
                                    last = mm(o[:, a, :], w[:, k, a * P:(a + 1) * P], ynT[:, k, :], start=k == 0, stop=False)
                                if a == 1:
                                    last.then_inc(s_slab, 1)
                                for k in range(6):
                                    last = mm(o[:, a, :], w2[:, k, a * P:(a + 1) * P], ynT[:, 6 + k, :], start=False, stop=k == 5)
                            last.then_inc(s_slab, 1)
                        for k in range(KD):
                            pe.wait_ge(t_gd.sem, t_gd.at(m, k + 1))
                            last = mm(psum[:, 3 + k // 4, (k % 4) * P:(k % 4 + 1) * P], ones, lnx[:, 0, k * P:(k + 1) * P], start=True, stop=True)
                        last.then_inc(t_gp.sem, 1)
                        pe.wait_ge(t_mT.sem, t_mT.at(m, 4))
                        for j in range(4):
                            token_major("wo", j, mT, SW)

                z, nt = e[l], len(MOE_TILES[l])
                for i in range(nt):
                    pe.wait_ge(s["u2_normed"], of(l, "u2_normed", i + 1))
                    if i:
                        pe.wait_ge(s["u2_ready"], of(l, "u2_ready", i))
                    for k in range(KD):
                        last = tp(psum[:, 3 + k // 4, (k % 4) * P:(k % 4 + 1) * P], ln2x[:, i % 2, k * P:(k + 1) * P], ident)
                    last.then_inc(s["u2_transposed"], 1)
                    pe.wait_ge(s["u2_ready"], of(l, "u2_ready", i + 1))
                    if i == 0:
                        pe.wait_ge(s["router_in"], of(l, "router_in", 32))
                    else:
                        pe.wait_ge(s["routed"], of(l, "routed", i))
                        pe.wait_ge(s["back_copied"], of(l, "back_copied", i))
                    for k in range(KD):
                        last = mm(bank[2][:, 0:NE], u2T[:, k, i * P:(i + 1) * P], rw[:, k, :], start=k == 0, stop=k == KD - 1)
                    last.then_inc(s["logits"], 1)
                    for k in range(KD):
                        last = tp(psum[:, 5 + k // 4, (k % 4) * P:(k % 4 + 1) * P], u2T[:, k, i * P:(i + 1) * P], ident)
                    last.then_inc(s["back_tp"], 1)
                pe.wait_ge(s["routed"], of(l, "routed", nt))
                for i in range(nt):
                    for b in range(i):
                        mm(bank[7][:, i * NE:(i + 1) * NE], ones, msk[:, b, :], start=b == 0, stop=False)
                    last = mm(bank[7][:, i * NE:(i + 1) * NE], tri_lt, msk[:, i, :], start=i == 0, stop=True)
                for b in range(nt):
                    last = mm(bank[7][:, 4 * NE:5 * NE], ones, msk[:, b, :], start=b == 0, stop=b == nt - 1)
                last.then_inc(s["counted"], 1)
                pe.wait_ge(s["shared_in"], of(l, "shared_in", 48))
                pe.wait_ge(s["back_copied"], of(l, "back_copied", nt))

                def up(o, lhs, w):
                    for k in range(KD):
                        last = mm(o, lhs(k), w[:, k, :], start=k == 0, stop=k == KD - 1)
                    return last

                def h_transpose(src):
                    tp(bank[4][:, 0:P], src[:, 0:P], ident)
                    return tp(bank[4][:, P:2 * P], src[:, P:2 * P], ident)

                def down(src, w):
                    for half in range(2):
                        for k in range(2):
                            last = mm(bank[5 + half][:, :], src[:, k, :], w[:, k, half * 512:(half + 1) * 512], start=k == 0, stop=k == 1)
                    return last

                for i in range(nt):
                    up(bank[i % 2], lambda k: u2T[:, k, i * P:(i + 1) * P], w13[2]).then_inc(s["shared_up"], 1)
                    if i == 0:
                        pe.wait_ge(s["placed"], of(l, "placed", 1))
                        tp(bank[7][0:1, 0:P], ecol[:, 0:1], ident).then_inc(s["rank_tp"], 1)
                    pe.wait_ge(s["shared_h"], of(l, "shared_h", i + 1))
                    h_transpose(hh[i % 2]).then_inc(s["shared_ht"], 1)
                    pe.wait_ge(s["shared_htc"], of(l, "shared_htc", i + 1))
                    if i:
                        pe.wait_ge(s["shared_out"], of(l, "shared_out", i))
                    down(hT[i % 2], w2s[2]).then_inc(s["shared_y"], 1)
                for v in range(nt // 2):
                    for k in range(KD):
                        pe.wait_ge(s["g2_diag"], of(l, "g2_diag", v * KD + k + 1))
                        last = mm(psum[:, 2 + k // 4, (k % 4) * P:(k % 4 + 1) * P], ones, ln2x[:, v, k * P:(k + 1) * P], start=True, stop=True)
                    last.then_inc(s["g2_rows"], 1)
                    pe.wait_ge(s["g2_ready"], of(l, "g2_ready", v + 1))
                pe.wait_ge(s["shared_out"], of(l, "shared_out", nt))
                pe.sem_inc(z["down"], 3)
                pe.sem_inc(z["up"], 2)
                pe.sem_inc(z["xt_tp"], 3)
                pe.sem_inc(z["ht_tp"], 2)
                pe.wait_ge(s["blocks_ready"], of(l, "blocks_ready", 1))
                n = pe.value_load(bexp[0:1, P:P + 1], min_val=1, max_val=NB)

                def x_transpose(i, b3, rounds):
                    pe.wait_ge(e_g[l][b3], rounds * 16)
                    pe.wait_ge(z["xt_act"], i + 1)
                    pe.wait_ge(z["xt_dve"], i + 1)
                    for k in range(KD):
                        last = tp(psum[:, 2 + k // 4, (k % 4) * P:(k % 4 + 1) * P], xg[b3][:, k * P:(k + 1) * P], ident)
                    last.then_inc(z["xt_tp"], 1)

                def block_up(i, b2, b3, rounds):
                    pe.wait_ge(z["xt_act"], i + 2)
                    pe.wait_ge(z["xt_dve"], i + 2)
                    pe.wait_ge(e_w[l][b3], rounds * 48)
                    pe.wait_ge(z["h_ready"], i + 1)
                    up(bank[b2], lambda k: xTe[b2][:, k, :], w13[b3]).then_inc(z["up"], 1)

                def block_down(i, b2, b3):
                    pe.wait_ge(z["h_ready"], i + 3)
                    pe.wait_ge(z["ht_copied"], i + 1)
                    h_transpose(hh[b2]).then_inc(z["ht_tp"], 1)
                    pe.wait_ge(z["ht_copied"], i + 2)
                    pe.wait_ge(z["y_act"], i + 1)
                    pe.wait_ge(z["y_dve"], i + 1)
                    down(hT[b2], w2s[b3]).then_inc(z["down"], 1)

                x_transpose(0, 0, 1)
                x_transpose(1, 1, 1)
                block_up(0, 0, 0, 1)
                with pe.Fori(0, NB // UNR) as ii:
                    for u in range(UNR):
                        i = ii * UNR + u
                        with pe.If(n > i + 2):
                            x_transpose(i + 2, (u + 2) % 3, ii * 2 + (u + 2) // 3 + 1)
                        with pe.If(n > i + 1):
                            block_up(i + 1, (u + 1) % 2, (u + 1) % 3, ii * 2 + (u + 1) // 3 + 1)
                        with pe.If(n > i):
                            block_down(i, u % 2, u % 3)

        @block.scalar
        def _(act):
            a_ = nc.scalar.activation
            count = {"chain": 0, "ln": 0}

            def link(ins_):
                count["chain"] += 1
                ins_.then_inc(s_achain, 1)
                act.wait_ge(s_achain, count["chain"])

            def ln_std(k=1):
                count["ln"] += 1
                act.wait_ge(s_var, count["ln"])
                a_(rstd[:, 0:1], mv[:, 1:2], ACT.Sqrt, bias=epsc[:, 0:1]).then_inc(s_std, 1)

            act.wait_ge(s_c, 32)
            for v in range(2):
                last = a_(csil[:, :, v], craw[:, v, :], ACT.Silu)
            last.then_inc(s_csil, 1)
            act.sem_inc(s_ada_row, 2)
            for l in range(DEPTH):
                act.wait_ge(s_tp_par, l + 1)
                a_(par[:, :], bank[7][:, 0:180], ACT.Copy).then_inc(s_parc, 1)
                act.wait_ge(s_par, 16 * 7 * (l + 1))
                link(a_(aneg[:, :], hpar[:, 48:96], ACT.Exp))
                a_(aneg[:, :], aneg[:, :], ACT.Copy, scale=-1.0).then_inc(s_parc, 1)
                with act.Fori(0, 6) as i:
                    for b in range(4):
                        act.wait_ge(s_ada_mm, i * 4 + b + 5 + 28 * l)
                        act.wait_ge(s_ada_col, i * 4 + b + 1 + 24 * l)
                        a_(modrow[:, b % 2, :], bank[b % 2][0:2, 0:SW], ACT.Copy).then_inc(s_ada_row, 1)

                for m, (cl, stream, full) in enumerate(CALLS):
                    if cl != l:
                        continue
                    act.wait_ge(s_modc, l + 1)
                    for t in range(NT):
                        ln_std()
                    for t in range(NT):
                        act.wait_ge(t_utp.sem, t_utp.at(m, t + 1))
                        for k in range(KD):
                            last = a_(uT[:, k, t * P:(t + 1) * P], psum[:, 3 + 2 * t + k // 4, (k % 4) * P:(k % 4 + 1) * P],
                                      ACT.Identity, scale=modc[:, 8 + k, stream:stream + 1], bias=modc[:, k, stream:stream + 1])
                        last.then_inc(t_uT.sem, 1)

                    def product(kind, j):
                        s_ = (m, kind, j)
                        act.wait_ge(s_slab, SLAB_NO[s_] + 1)
                        return bank[BANK_NO[s_] % 2]

                    def conv_silu(j):
                        act.wait_ge(t_cv.sem, t_cv.at(m, j + 1))
                        if j < 6 and j >= 2:
                            act.wait_ge(t_ctp.sem, t_ctp.at(m, j - 1))
                        for a in range(2):
                            ch = 2 * j + a
                            if ch < XT_TILES:
                                dst = cxt[:, ch % 4, :]
                            elif ch < XT_TILES + GROUPS:
                                dst = bT[:, ch - XT_TILES, :]
                            else:
                                dst = cT[:, ch - XT_TILES - GROUPS, :]
                            last = a_(dst, cacc[:, ch % 4, :], ACT.Silu)
                        last.then_inc(t_cs.sem, 1)

                    def conv_out(j):
                        act.wait_ge(t_ctp.sem, t_ctp.at(m, j + 1))
                        src = bank[2 + 5 * (j % 2)].rearrange("p (c n) -> p c n", c=NT)
                        dst = xs[:, :, j * SW:(j + 1) * SW] if j < 6 else btok[:, :, (j - 6) * SW:(j - 5) * SW]
                        a_(dst, src, ACT.Copy).then_inc(t_xs.sem, 1)

                    if full:
                        for j in range(4):
                            src = product("four", j)
                            a_(fT[:, 2 * j:2 * j + 2, :], src.rearrange("p (a t) -> p a t", a=2), ACT.Copy).then_inc(s_read["act"], 1)
                    act.wait_ge(t_dtr.sem, t_dtr.at(m, 1))
                    a_(sp[1], sp[0], ACT.Exp, scale=-1.0).then_inc(t_dtx.sem, 1)
                    nx = 10 if full else 8
                    for j in range(nx):
                        src = product("xbc", j)
                        if j >= 2:
                            act.wait_ge(t_cs.sem, t_cs.at(m, j - 1))
                        for a in range(2):
                            ch = 2 * j + a
                            last = a_(cacc[:, ch % 4, :], src[:, a * SEQ:(a + 1) * SEQ], ACT.Identity,
                                      scale=par[:, 60 + 2 * 20 + ch:61 + 2 * 20 + ch], bias=par[:, 160 + ch:161 + ch])
                        last.then_inc(t_acc.sem, 1)
                        if j >= 1:
                            conv_silu(j - 1)
                        if 3 <= j:
                            conv_out(j - 3)
                    conv_silu(nx - 1)
                    conv_out(nx - 3) if nx == 10 else conv_out(5)
                    if nx == 8:
                        conv_out(6)
                        conv_out(7)
                    act.wait_ge(t_acu.sem, t_acu.at(m, 1))
                    a_(eac[:, :, :], acu[:, :, 0:48], ACT.Exp)
                    a_(ecd[:, :, :], acu[:, :, 48:96], ACT.Exp)
                    a_(sp[3], sp[2], ACT.Exp).then_inc(t_eac.sem, 1)
                    if full:
                        for j in range(6):
                            src = product("z", j)
                            a_(zs[:, :, j * SW:(j + 1) * SW], src.rearrange("p (c n) -> p c n", c=NT), ACT.Silu).then_inc(s_read["act"], 1)
                        for g in range(GROUPS + 1):
                            if g < GROUPS:
                                act.wait_ge(t_f1.sem, t_f1.at(m, g + 1))
                                if g >= 2:
                                    act.wait_ge(t_f2.sem, t_f2.at(m, g - 1))
                                a_(fA[:, g % 2, :, :], psum[:, 3:5, :], ACT.Copy).then_inc(t_f1c.sem, 1)
                            if g:
                                act.wait_ge(t_f2.sem, t_f2.at(m, g))
                                a_(fO[:, 2 * g - 2:2 * g, :], bank[6].rearrange("p (a t) -> p a t", a=2), ACT.Copy).then_inc(t_f2c.sem, 1)
                        for it in range(8):
                            act.wait_ge(t_seg.sem, t_seg.at(m, it + 1))
                            a_(seg[:, :, :, :], seg[:, :, :, :], ACT.Exp).then_inc(t_exp.sem, 1)
                            if it % 2 == 0:
                                j = it // 2
                                src = product("g2", j)
                                a_(gT[:, 2 * j:2 * j + 2, :], src.rearrange("p (a t) -> p a t", a=2), ACT.Sigmoid).then_inc(s_read["act"], 1)
                        for c in range(NT):
                            act.wait_ge(t_h.sem, t_h.at(m, c + 1))
                            act.wait_ge(t_y.sem, t_y.at(m, 8))
                            link(a_(seg[:, :, :, :].rearrange("p d h l -> p (d h l)"), zs[:, c, :], ACT.Square, accum_out=rss[:, c, 0:1]))
                        for c in range(NT):
                            last = a_(rss[:, c, 1:2], rss[:, c, 0:1], ACT.Sqrt, scale=1.0 / DIN, bias=epsc[:, 0:1])
                            last.then_inc(t_ss.sem, 1)
                        for j in range(4):
                            src = product("g1", j)
                            act.wait_ge(t_mT2.sem, t_mT2.at(m, 4))
                            a_(gT[:, 2 * j:2 * j + 2, :], src.rearrange("p (a t) -> p a t", a=2), ACT.Sigmoid).then_inc(s_read["act"], 1)
                        for c in range(NT):
                            for b in range(3):
                                k = 3 * c + b
                                act.wait_ge(t_ytp.sem, t_ytp.at(m, k + 1))
                                for a in range(4):
                                    ch = 4 * b + a
                                    last = a_(ynT[:, ch, c * P:(c + 1) * P], bank[2 + 5 * (k % 2)][:, a * P:(a + 1) * P], ACT.Copy,
                                              scale=par[:, 48 + ch:49 + ch])
                                last.then_inc(t_yT.sem, 1)
                        act.wait_ge(t_gp.sem, t_gp.at(m, 1))
                        a_(grow[:, 0, :], psum[:, 3:5, :].rearrange("p b n -> p (b n)"), ACT.Copy).then_inc(t_gr.sem, 1)
                        for t in range(NT):
                            ln_std()

                z, nt = e[l], len(MOE_TILES[l])
                for i in range(nt):
                    ln_std()
                    v = MOE_TILES[l][i] // 2
                    act.wait_ge(s["u2_transposed"], of(l, "u2_transposed", i + 1))
                    for k in range(KD):
                        last = a_(u2T[:, k, i * P:(i + 1) * P], psum[:, 3 + k // 4, (k % 4) * P:(k % 4 + 1) * P],
                                  ACT.Identity, scale=modc[:, 32 + k, v:v + 1], bias=modc[:, 24 + k, v:v + 1])
                    last.then_inc(s["u2_ready"], 1)
                    act.wait_ge(s["logits"], of(l, "logits", i + 1))
                    a_(rt[0][:, :], bank[2][:, 0:NE], ACT.Sigmoid).then_inc(s["scores"], 1)
                    act.wait_ge(s["back_tp"], of(l, "back_tp", i + 1))
                    a_(macc[:, i, :], psum[:, 5:7, :].rearrange("p b n -> p (b n)"), ACT.Copy).then_inc(s["back_copied"], 1)
                    act.wait_ge(s["routed"], of(l, "routed", i + 1))
                for i in range(nt):
                    act.wait_ge(s["shared_up"], of(l, "shared_up", i + 1))
                    if i >= 2:
                        act.wait_ge(s["shared_h"], of(l, "shared_h", i - 1))
                    a_(hs[i % 2], bank[i % 2][:, 0:FF], ACT.Silu).then_inc(s["shared_sil"], 1)
                    act.wait_ge(s["shared_y"], of(l, "shared_y", i + 1))
                    if i == 0:
                        act.wait_ge(s["u2_stored"], of(l, "u2_stored", 16 * nt))
                    a_(macc[:, i, :], psum[:, 5:7, :].rearrange("p b n -> p (b n)"), ACT.Copy).then_inc(s["shared_out"], 1)
                act.sem_inc(z["xt_act"], 1)
                act.sem_inc(z["y_act"], 1)
                act.wait_ge(s["blocks_ready"], of(l, "blocks_ready", 1))
                n = act.value_load(bexp[0:1, P:P + 1], min_val=1, max_val=NB)

                def x_copy(i, b2):
                    act.wait_ge(z["xt_tp"], i + 4)
                    act.wait_ge(z["up"], i + 1)
                    a_(xTe[b2][:, 0:4, :], bank[2].rearrange("p (k t) -> p k t", k=4), ACT.Copy).then_inc(z["xt_act"], 1)

                x_copy(0, 0)
                x_copy(1, 1)
                with act.Fori(0, NB // UNR) as ii:
                    for u in range(UNR):
                        i = ii * UNR + u
                        with act.If(n > i):
                            act.wait_ge(z["up"], i + 3)
                            act.wait_ge(z["h_ready"], i + 1)
                            a_(hs[u % 2], bank[u % 2][:, 0:FF], ACT.Silu).then_inc(z["silu"], 1)
                        with act.If(n > i + 2):
                            x_copy(i + 2, u % 2)
                        with act.If(n > i):
                            act.wait_ge(z["down"], i + 4)
                            act.wait_ge(e_s[l][u % 2], 16 * (ii * 3 + u // 2 + 1))
                            a_(ysb[u % 2][:, 0:512], bank[5], ACT.Copy).then_inc(z["y_act"], 1)
                for i in range(nt):
                    ln_std()

        @block.vector
        def _(dve):
            V = nc.vector
            count = {"chain": 0, "ln": 0}

            def link(ins_):
                count["chain"] += 1
                ins_.then_inc(s_chain, 1)
                dve.wait_ge(s_chain, count["chain"])

            def norm(dst, src, last=None):
                for hlf in range(2):
                    i_ = V.bn_stats(stat[:, hlf, :], src[:, hlf * 512:(hlf + 1) * 512])
                link(i_)
                count["ln"] += 1
                V.bn_aggr(mv[:, :], stat[:, :, :].rearrange("p a b -> p (a b)")).then_inc(s_var, 1)
                dve.wait_ge(s_var, count["ln"])
                dve.wait_ge(s_std, count["ln"])
                link(V.reciprocal(rstd[:, 1:2], rstd[:, 0:1]))
                i_ = V.tensor_scalar(dst, src, mv[:, 0:1], rstd[:, 1:2], ALU.subtract, ALU.mult)
                if last is None:
                    link(i_)
                else:
                    i_.then_inc(last, 1)

            def post_norm(t, tmp, which):
                norm(tmp, tmp)
                dve.wait_ge(s_lnrow, 32 * (which + 1))
                link(V.tensor_tensor(tmp, tmp, lnrow[:, 0, :], ALU.mult))
                return V.tensor_tensor(xres[:, t, :], tmp, lnrow[:, 1, :], ALU.add)

            link(V.memset(epsc[:, :], EPS))
            dve.sem_inc(s_ada_col, 1)
            dve.wait_ge(s_const, 48)
            dve.wait_ge(s_x, 16 * 4)
            dve.wait_ge(s_pos, 32)
            for t in range(NT):
                link(V.tensor_tensor(xres[:, t, :], xres[:, t, :], lnx[:, t, :], ALU.add))
            which = 0
            for l in range(DEPTH):
                dve.wait_ge(s_parc, 2 * l + 2)
                with dve.Fori(0, 6) as i:
                    for b in range(4):
                        dve.wait_ge(s_ada_tp, i * 4 + b + 1 + 24 * l)
                        o = bass.ds(i * 8 + 2 * b, 2)
                        V.tensor_tensor(modc[:, o, :], bank[3][:, 0:4].rearrange("p (j v) -> p j v", j=2),
                                        par[:, o].unsqueeze(2).to_broadcast([P, 2, 2]), ALU.add).then_inc(s_ada_col, 1)
                dve.wait_ge(s_ada_col, 24 * (l + 1) + 1)
                link(V.tensor_scalar(modc[:, 8:16, :], modc[:, 8:16, :], 1.0, None, ALU.add))
                V.tensor_scalar(modc[:, 32:40, :], modc[:, 32:40, :], 1.0, None, ALU.add).then_inc(s_modc, 1)
                dve.wait_ge(s_modc, l + 1)

                for m, (cl, stream, full) in enumerate(CALLS):
                    if cl != l:
                        continue
                    for t in range(NT):
                        norm(lnx[:, t, :], xres[:, TILES[stream][t], :], t_lnx.sem)

                    def product(kind, j):
                        s_ = (m, kind, j)
                        dve.wait_ge(s_slab, SLAB_NO[s_] + 1)
                        return bank[BANK_NO[s_] % 2]

                    src = product("dt", 0).rearrange("p (c n) -> p c n", c=NT)[:, :, 0:48]
                    bias = hpar[:, 0:48].unsqueeze(1).to_broadcast([P, NT, 48])
                    V.tensor_tensor(sp[2], src, bias, ALU.add).then_inc(s_read["dve"], 1)
                    dve.wait_ge(s_read["dve"], freed(BANK_NO[(m, "dt", 0)])[1])
                    link(V.tensor_scalar(sp[3], sp[2], -1.0, None, ALU.mult))
                    V.tensor_tensor(sp[0], sp[2], sp[3], ALU.max).then_inc(t_dtr.sem, 1)
                    dve.wait_ge(t_dtx.sem, t_dtx.at(m, 1))
                    link(V.tensor_scalar(sp[3], sp[1], 2.0, None, ALU.add))
                    link(V.reciprocal(sp[3], sp[3]))
                    link(V.tensor_tensor(sp[1], sp[1], sp[3], ALU.mult))
                    link(V.tensor_tensor(sp[3], sp[1], sp[1], ALU.mult))
                    link(V.tensor_scalar(sp[0], sp[3], 2.0 / 17, 2.0 / 15, ALU.mult, ALU.add))
                    for d_ in (13, 11, 9, 7, 5, 3, 1):
                        link(V.tensor_tensor(sp[0], sp[0], sp[3], ALU.mult))
                        link(V.tensor_scalar(sp[0], sp[0], 2.0 / d_, None, ALU.add))
                    link(V.tensor_tensor(sp[0], sp[0], sp[1], ALU.mult))
                    link(V.tensor_scalar(sp[2], sp[2], 0.0, None, ALU.max))
                    link(V.tensor_tensor(dtv[:, :, :], sp[0], sp[2], ALU.add))
                    V.tensor_tensor(adt[:, :, :], dtv[:, :, :], aneg[:, :].unsqueeze(1).to_broadcast([P, NT, 48]), ALU.mult).then_inc(t_adt.sem, 1)

                    for j in range(10 if full else 8):
                        src = product("xbc", j)
                        dve.wait_ge(t_acc.sem, t_acc.at(m, j + 1))
                        for tap in (0, 1, 3, 4):
                            sh = tap - CONVW // 2
                            lo, hi = max(0, -sh), min(SEQ, SEQ - sh)
                            for a in range(2):
                                ch = 2 * j + a
                                dst = cacc[:, ch % 4, lo:hi]
                                i_ = V.scalar_tensor_tensor(dst, src[:, a * SEQ + lo + sh:a * SEQ + hi + sh],
                                                            par[:, 60 + tap * 20 + ch:61 + tap * 20 + ch], dst, ALU.mult, ALU.add)
                                if tap == 4 and a == 1:
                                    i_.then_inc(t_cv.sem, 1)
                                    dve.wait_ge(t_cv.sem, t_cv.at(m, j + 1))
                                elif a == 1 or tap == 4:
                                    link(i_)
                        dve.sem_inc(s_read["dve"], 1)

                    dve.wait_ge(t_acp.sem, t_acp.at(m, 1))
                    link(V.tensor_copy(acu[:, :, :], bank[5][:, 0:NT * 96].rearrange("p (c n) -> p c n", c=NT)))
                    V.tensor_tensor(sp[2], acu[:, :, 48:96], acu[:, :, 0:48], ALU.subtract).then_inc(t_acu.sem, 1)
                    dve.wait_ge(t_eac.sem, t_eac.at(m, 1))
                    V.tensor_tensor(dec[:, :, :], sp[3], dtv[:, :, :], ALU.mult).then_inc(t_dec.sem, 1)
                    dve.wait_ge(t_xs.sem, t_xs.at(m, 6))
                    dve.wait_ge(t_dec.sem, t_dec.at(m, 1))

                    def state_round(i, d, c, g, dst, prev):
                        if i >= 2:
                            dve.wait_ge(t_stp.sem, t_stp.at(m, i - 1))
                        h0 = d * HEADS + g * HPG
                        V.tensor_tensor(wst[:, i % 2, :].rearrange("p (h d) -> p h d", h=HPG),
                                        xs[:, c, g * GW:(g + 1) * GW].rearrange("p (h d) -> p h d", h=HPG),
                                        dec[:, c, h0:h0 + HPG].unsqueeze(2).to_broadcast([P, HPG, HD]), ALU.mult).then_inc(t_w.sem, 1)

                    def state_add(i, d, c, g, dst, prev):
                        dve.wait_ge(t_stp.sem, t_stp.at(m, i + 1))
                        h0 = d * HEADS + g * HPG
                        src = bank[5 + i % 2][:, 0:GW].rearrange("p (h d) -> p h d", h=HPG)
                        hsl = slice(g * HPG, (g + 1) * HPG)
                        if prev is None:
                            V.tensor_copy(dst[:, hsl, :], src).then_inc(t_st.sem, 1)
                        else:
                            link(V.tensor_tensor(dst[:, hsl, :], prev[:, hsl, :],
                                                 ecd[:, c, h0:h0 + HPG].unsqueeze(2).to_broadcast([P, HPG, HD]), ALU.mult))
                            V.tensor_tensor(dst[:, hsl, :], dst[:, hsl, :], src, ALU.add).then_inc(t_st.sem, 1)

                    def state_pass(lst, base):
                        for i, a_ in enumerate(lst):
                            state_round(base + i, *a_)
                            if i:
                                state_add(base + i - 1, *lst[i - 1])
                        state_add(base + len(lst) - 1, *lst[-1])

                    init = stream == 1
                    state_pass([(0, 0, g, st[0][1], None if init else st[0][0]) for g in range(4)]
                               + [(1, 1, g, st[1][1], None if init else st[1][0]) for g in range(4)], 0)

                    if full:
                        dsk = hpar[:, 96:120]

                        def head(it):
                            c, g = it // GROUPS, it % GROUPS
                            if it:
                                dve.wait_ge(t_y.sem, t_y.at(m, it))
                            for d in range(2):
                                dve.wait_ge(t_row.sem, t_row.at(m, 2 * it + d + 1))
                                h0 = d * HEADS + g * HPG
                                src = psum[:, 3:5, :].rearrange("p b n -> p (b n)")
                                if d == 0:
                                    link(V.tensor_tensor(smask[:, 0, :], src[:, 768:896], tri_le, ALU.mult))
                                    V.tensor_tensor(smask[:, 1, :], src[:, 768:896], tri_ge, ALU.mult).then_inc(t_sm.sem, 1)
                                V.tensor_tensor(seg[:, d, :, :], src[:, 0:768].rearrange("p (h l) -> p h l", h=HPG),
                                                acu[:, c, h0:h0 + HPG].unsqueeze(2).to_broadcast([P, HPG, P]), ALU.subtract).then_inc(t_rowr.sem, 1)
                            dve.wait_ge(t_rowr.sem, t_rowr.at(m, 2 * it + 2))
                            V.tensor_scalar(seg[:, :, :, :], seg[:, :, :, :], 0.0, None, ALU.min).then_inc(t_seg.sem, 1)

                        def weigh(it):
                            dve.wait_ge(t_exp.sem, t_exp.at(m, it + 1))
                            dve.wait_ge(t_sm.sem, t_sm.at(m, it + 1))
                            V.tensor_tensor(seg[:, 0, :, :], seg[:, 0, :, :], smask[:, 0, :].unsqueeze(1).to_broadcast([P, HPG, P]), ALU.mult).then_inc(t_lmF.sem, 1)

                        def merge_four(j):
                            src = product("bf", j)
                            dve.wait_ge(s_read["act"], freed(BANK_NO[(m, "g2", j)])[1])
                            V.tensor_tensor(mT[:, 2 * j:2 * j + 2, :], gT[:, 2 * j:2 * j + 2, :], src.rearrange("p (a t) -> p a t", a=2), ALU.mult).then_inc(s_read["dve"], 1)
                            dve.wait_ge(s_read["dve"], freed(BANK_NO[(m, "bf", j)])[1])
                            dve.sem_inc(t_mT2.sem, 1)

                        def tail(it):
                            c, g = it // GROUPS, it % GROUPS
                            dve.wait_ge(t_y.sem, t_y.at(m, it + 1))
                            xv = xs[:, c, g * GW:(g + 1) * GW].rearrange("p (h d) -> p h d", h=HPG)
                            v3 = lambda a: a.rearrange("p (h d) -> p h d", h=HPG)
                            hb = lambda a: a.unsqueeze(2).to_broadcast([P, HPG, HD])
                            y0, y1, y2 = (ytmp[:, b, :] for b in range(3))
                            link(V.tensor_tensor(v3(y0), xv, hb(dsk[:, g * HPG:(g + 1) * HPG]), ALU.mult))
                            link(V.tensor_tensor(y0, y0, bank[5][:, 0:GW], ALU.add))
                            for d in range(2):
                                w_ = c if d == 0 else 1 - c
                                if stream == 0 or w_ == 1:
                                    h0 = d * HEADS + g * HPG
                                    link(V.tensor_tensor(v3(y1), v3(bank[6 + d][:, 0:GW]), hb(eac[:, c, h0:h0 + HPG]), ALU.mult))
                                    link(V.tensor_tensor(y0, y0, y1, ALU.add))
                            dve.sem_inc(t_yr.sem, 1)
                            zz = zs[:, c, g * GW:(g + 1) * GW]
                            dve.wait_ge(s_read["act"], freed(BANK_NO[(m, "z", 5)])[1])
                            i_ = V.tensor_tensor(zz, y0, zz, ALU.mult)
                            if g == GROUPS - 1:
                                i_.then_inc(t_h.sem, 1)

                        for it in range(8):
                            head(it)
                            if it:
                                tail(it - 1)
                            weigh(it)
                            if it % 2 == 0 and it:
                                merge_four(it // 2 - 1)
                        merge_four(3)
                        tail(7)

                    if stream == 1:
                        if full:
                            dve.wait_ge(t_y.sem, t_y.at(m, 8))
                        state_pass([(0, 1, g, st[0][0], st[0][1]) for g in range(4)]
                                   + [(1, 0, g, st[1][0], st[1][1]) for g in range(4)], 8)

                    if full:
                        for c in range(NT):
                            dve.wait_ge(t_ss.sem, t_ss.at(m, c + 1))
                        link(V.reciprocal(rss[:, :, 1], rss[:, :, 1]))
                        dve.wait_ge(t_h.sem, t_h.at(m, 2))
                        for c in range(NT):
                            V.tensor_scalar(zs[:, c, :], zs[:, c, :], rss[:, c, 1:2], None, ALU.mult).then_inc(t_yn.sem, 1)
                        for k in range(KD):
                            V.tensor_scalar(lnx[:, 0, k * P:(k + 1) * P], ident, modc[:, 16 + k, stream:stream + 1], None, ALU.mult).then_inc(t_gd.sem, 1)
                        for j in range(4):
                            dve.wait_ge(s_slab, SLAB_NO[(m, "bsb", j)] + 1)
                            dve.wait_ge(s_read["act"], freed(BANK_NO[(m, "g1", j)])[1])
                            src = bank[BANK_NO[(m, "bsb", j)] % 2].rearrange("p (a t) -> p a t", a=2)
                            g_ = gT[:, 2 * j:2 * j + 2, :]
                            V.tensor_tensor(g_, g_, src, ALU.mult).then_inc(s_read["dve"], 1)
                            dve.wait_ge(s_read["dve"], freed(BANK_NO[(m, "bsb", j)])[1])
                            V.tensor_tensor(mT[:, 2 * j:2 * j + 2, :], mT[:, 2 * j:2 * j + 2, :], g_, ALU.add).then_inc(t_mT.sem, 1)
                        dve.wait_ge(t_gr.sem, t_gr.at(m, 1))
                        for j in range(4):
                            src = product("wo", j).rearrange("p (c n) -> p c n", c=NT)
                            V.tensor_tensor(yrow[:, :, :], src, grow[:, 0, j * SW:(j + 1) * SW].unsqueeze(1).to_broadcast([P, NT, SW]), ALU.mult).then_inc(s_read["dve"], 1)
                            dve.wait_ge(s_read["dve"], freed(BANK_NO[(m, "wo", j)])[1])
                            t0 = TILES[stream][0]
                            xv = xres[:, t0:t0 + NT, j * SW:(j + 1) * SW]
                            link(V.scalar_tensor_tensor(xv, xv, ALPHA, yrow[:, :, :], ALU.mult, ALU.add))
                        for t in range(NT):
                            i_ = post_norm(TILES[stream][t], xres[:, TILES[stream][t], :], which)
                            if t == NT - 1:
                                i_.then_inc(s_lnrow_free, 1)
                                dve.wait_ge(s_lnrow_free, which + 1)
                            else:
                                link(i_)
                        which += 1

                z, nt = e[l], len(MOE_TILES[l])
                for b in range(3):
                    link(V.memset(xg[b], 0.0))
                big = 3.0e38
                sc, sel, s3, mk, cum, pos, pend, base = rt
                for i in range(nt):
                    if i >= 2:
                        dve.wait_ge(s["u2_transposed"], of(l, "u2_transposed", i - 1))
                    norm(ln2x[:, i % 2, :], xres[:, MOE_TILES[l][i], :], s["u2_normed"])
                    dve.wait_ge(s["scores"], of(l, "scores", i + 1))
                    dve.wait_ge(s["router_in"], of(l, "router_in", 32))
                    link(V.tensor_tensor(sel, sc, rbias, ALU.add))
                    g3 = sel.rearrange("p (g e) -> p g e", g=NGRP)
                    for g in range(NGRP):
                        link(V.max(r8[1], sel[:, g * EPG:(g + 1) * EPG]))
                        link(V.tensor_tensor(r8[2][:, g:g + 1], r8[1][:, 0:1], r8[1][:, 1:2], ALU.add))
                    sq = lambda v_: v_.rearrange("p (g e) -> p g e", g=NGRP)
                    other = r8[2].unsqueeze(1).to_broadcast([P, NGRP, NGRP])
                    own = r8[2].unsqueeze(2).to_broadcast([P, NGRP, NGRP])
                    link(V.tensor_tensor(sq(mk), other, own, ALU.is_equal))
                    link(V.tensor_tensor(mk, mk, cst[:, C_TRI8:C_TRI8 + NGRP * NGRP], ALU.mult))
                    link(V.tensor_tensor(sq(cum), other, own, ALU.is_gt))
                    link(V.tensor_tensor(mk, mk, cum, ALU.add))
                    link(V.tensor_reduce(r8[1], sq(mk), AX.X, ALU.add))
                    link(V.tensor_scalar(r8[3], r8[1], float(TOPG), None, ALU.is_lt))
                    link(V.tensor_scalar(r8[0], r8[3], big, -big, ALU.mult, ALU.add))
                    gsel = r8[3].unsqueeze(2).to_broadcast([P, NGRP, EPG])
                    gneg = r8[0].unsqueeze(2).to_broadcast([P, NGRP, EPG])
                    link(V.tensor_tensor(s3.rearrange("p (g e) -> p g e", g=NGRP), g3, gsel, ALU.mult))
                    link(V.tensor_tensor(s3.rearrange("p (g e) -> p g e", g=NGRP), s3.rearrange("p (g e) -> p g e", g=NGRP), gneg, ALU.add))
                    link(V.max(r8[1], s3))
                    link(V.match_replace(mk, r8[1], s3, big))
                    link(V.tensor_scalar(msk[:, i, :], mk, big, None, ALU.is_equal))
                    link(V.tensor_tensor_scan(cum, ones[:, 0:NE], msk[:, i, :], 0.0, ALU.mult, ALU.add))
                    link(V.tensor_tensor(cum, cum, msk[:, i, :], ALU.mult))
                    link(V.tensor_scalar(cum, cum, -1.0, None, ALU.add))
                    c3 = cube.rearrange("p (j e) -> p j e", j=TOPK)
                    link(V.tensor_tensor(c3, cst[:, C_RANK:C_RANK + TOPK * NE].rearrange("p (j e) -> p j e", j=TOPK),
                                         cum.unsqueeze(1).to_broadcast([P, TOPK, NE]), ALU.is_equal))
                    link(V.tensor_tensor(c3, c3, sc.unsqueeze(1).to_broadcast([P, TOPK, NE]), ALU.mult))
                    link(V.tensor_reduce(gat[:, i, :], c3, AX.X, ALU.add))
                    link(V.tensor_reduce(r8[0][:, 0:1], gat[:, i, :], AX.X, ALU.add))
                    link(V.reciprocal(r8[0][:, 0:1], r8[0][:, 0:1]))
                    V.tensor_scalar(gat[:, i, :], gat[:, i, :], r8[0][:, 0:1], 2.5, ALU.mult, ALU.mult).then_inc(s["routed"], 1)
                    dve.wait_ge(s["routed"], of(l, "routed", i + 1))
                dve.wait_ge(s["counted"], of(l, "counted", 1))
                cnt = bank[7][:, 4 * NE:5 * NE]
                link(V.tensor_scalar(mk, cnt, 0.0, None, ALU.is_gt))
                for k in range(1, nt):
                    link(V.scalar_tensor_tensor(mk, cnt, float(k * P), mk, ALU.is_gt, ALU.add))
                link(V.tensor_tensor_scan(pend, ones[:, 0:NE], mk, 0.0, ALU.mult, ALU.add))
                link(V.tensor_tensor(base, pend, mk, ALU.subtract))
                for i in range(nt):
                    ps = bank[7][:, i * NE:(i + 1) * NE]
                    link(V.tensor_scalar(s3, ps, float(P), None, ALU.is_ge))
                    for k in range(2, nt):
                        link(V.scalar_tensor_tensor(s3, ps, float(k * P), s3, ALU.is_ge, ALU.add))
                    link(V.scalar_tensor_tensor(pos, s3, -float(P), ps, ALU.mult, ALU.add))
                    link(V.scalar_tensor_tensor(pos, pos, float(NB), s3, ALU.mult, ALU.add))
                    link(V.tensor_tensor(pos, pos, base, ALU.add))
                    link(V.tensor_tensor_scan(cum, ones[:, 0:NE], msk[:, i, :], 0.0, ALU.mult, ALU.add))
                    link(V.tensor_tensor(cum, cum, msk[:, i, :], ALU.mult))
                    link(V.tensor_scalar(cum, cum, -1.0, None, ALU.add))
                    c3 = cube.rearrange("p (j e) -> p j e", j=TOPK)
                    link(V.tensor_tensor(c3, cst[:, C_RANK:C_RANK + TOPK * NE].rearrange("p (j e) -> p j e", j=TOPK),
                                         cum.unsqueeze(1).to_broadcast([P, TOPK, NE]), ALU.is_equal))
                    link(V.tensor_tensor(c3, c3, pos.unsqueeze(1).to_broadcast([P, TOPK, NE]), ALU.mult))
                    link(V.tensor_reduce(slotf[:, i, :], c3, AX.X, ALU.add))
                    link(V.tensor_copy(sloti[:, i, :], slotf[:, i, :]))
                    link(V.tensor_scalar(slotf[:, i, :], cst[:, C_TOK:C_TOK + TOPK], float(i * P * TOPK), None, ALU.add))
                    V.tensor_copy(tokid[:, i, :], slotf[:, i, :]).then_inc(s["table_ready"], 1)
                    dve.wait_ge(s["table_ready"], of(l, "table_ready", i + 1))
                link(V.tensor_scalar(s3, pend, cst[:, C_P:C_P + 1], None, ALU.is_le))
                link(V.tensor_reduce(ecol[:, :], s3, AX.X, ALU.add))
                V.tensor_scalar(ecol[:, :], ecol[:, :], float(NE - 1), None, ALU.min).then_inc(s["placed"], 1)
                link(V.tensor_copy(bexp[0:1, P:P + 1], pend[0:1, NE - 1:NE]))
                dve.wait_ge(s["rank_tp"], of(l, "rank_tp", 1))
                V.tensor_copy(bexp[0:1, 0:P], bank[7][0:1, 0:P]).then_inc(s["blocks_ready"], 1)
                dve.wait_ge(s["blocks_ready"], of(l, "blocks_ready", 1))
                for i in range(nt):
                    dve.wait_ge(s["shared_sil"], of(l, "shared_sil", i + 1))
                    V.tensor_tensor(hh[i % 2], hs[i % 2], bank[i % 2][:, FF:2 * FF], ALU.mult).then_inc(s["shared_h"], 1)
                    dve.wait_ge(s["shared_ht"], of(l, "shared_ht", i + 1))
                    V.tensor_copy(hT[i % 2], bank[4][:, 0:2 * P].rearrange("p (k t) -> p k t", k=2)).then_inc(s["shared_htc"], 1)
                for v in range(nt // 2):
                    for k in range(KD):
                        V.tensor_scalar(ln2x[:, v, k * P:(k + 1) * P], ident, modc[:, 40 + k, v:v + 1], None, ALU.mult).then_inc(s["g2_diag"], 1)
                    dve.wait_ge(s["g2_rows"], of(l, "g2_rows", v + 1))
                    V.tensor_copy(grow[:, v, :], psum[:, 2:4, :].rearrange("p b n -> p (b n)")).then_inc(s["g2_ready"], 1)
                dve.wait_ge(s["g2_ready"], of(l, "g2_ready", nt // 2))
                dve.wait_ge(s["table_in"], of(l, "table_in", 16))
                V.tensor_scalar(tblg[:, 0:NB], tbl[:, 0:NB], 3, None, ALU.logical_shift_right).then_inc(s_shift[l], 1)
                dve.sem_inc(z["xt_dve"], 1)
                dve.sem_inc(z["y_dve"], 1)
                dve.sem_inc(z["h_ready"], 2)
                dve.sem_inc(z["ht_copied"], 1)
                n = dve.value_load(bexp[0:1, P:P + 1], min_val=1, max_val=NB)

                def x_copy(i, b2):
                    dve.wait_ge(z["xt_tp"], i + 4)
                    dve.wait_ge(z["up"], i + 1)
                    V.tensor_copy(xTe[b2][:, 4:8, :], bank[3].rearrange("p (k t) -> p k t", k=4)).then_inc(z["xt_dve"], 1)

                x_copy(0, 0)
                x_copy(1, 1)
                with dve.Fori(0, NB // UNR) as ii:
                    for u in range(UNR):
                        i = ii * UNR + u
                        with dve.If(n > i):
                            dve.wait_ge(z["silu"], i + 1)
                            dve.wait_ge(z["ht_tp"], i + 1)
                            V.tensor_tensor(hh[u % 2], hs[u % 2], bank[u % 2][:, FF:2 * FF], ALU.mult).then_inc(z["h_ready"], 1)
                        with dve.If(n > i + 2):
                            x_copy(i + 2, u % 2)
                        with dve.If(n > i):
                            dve.wait_ge(z["ht_tp"], i + 3)
                            dve.wait_ge(z["down"], i + 2)
                            V.tensor_copy(hT[u % 2], bank[4][:, 0:2 * P].rearrange("p (k t) -> p k t", k=2)).then_inc(z["ht_copied"], 1)
                            dve.wait_ge(z["down"], i + 4)
                            dve.wait_ge(e_s[l][u % 2], 16 * (ii * 3 + u // 2 + 1))
                            V.tensor_copy(ysb[u % 2][:, 512:1024], bank[6]).then_inc(z["y_dve"], 1)
                for i in range(nt):
                    t = MOE_TILES[l][i]
                    dve.wait_ge(s["shared_out"], of(l, "shared_out", i + 1))
                    dve.wait_ge(e_yin[l], 16 * (i + 1))
                    for j in range(TOPK):
                        link(V.scalar_tensor_tensor(macc[:, i, :], yall[:, j, :], gat[:, i, j:j + 1], macc[:, i, :], ALU.mult, ALU.add))
                    link(V.tensor_tensor(macc[:, i, :], macc[:, i, :], grow[:, t // 2, :], ALU.mult))
                    link(V.scalar_tensor_tensor(xres[:, t, :], xres[:, t, :], ALPHA, macc[:, i, :], ALU.mult, ALU.add))
                    i_ = post_norm(t, xres[:, t, :], which)
                    i_.then_inc(e_comb[l], 1)
                    dve.wait_ge(e_comb[l], i + 1)
                dve.sem_inc(s_lnrow_free, 1)
                which += 1

        @block.gpsimd
        def _(gp):
            G = nc.gpsimd
            count = {"chain": 0}

            def link(ins_):
                count["chain"] += 1
                ins_.then_inc(s_pchain, 1)
                gp.wait_ge(s_pchain, count["chain"])

            link(gp.memset(sent[:, :], SENTINEL))
            for l in range(DEPTH):
                z, nt = e[l], len(MOE_TILES[l])
                gp.dma_start(scratch["tbl"][l].rearrange("(p b) o -> p (b o)", b=NB), sent[:, :]).then_inc(s["sentinel_in"], 16)
                for m, (cl, stream, full) in enumerate(CALLS):
                    if cl != l or not full:
                        continue
                    gp.wait_ge(t_xs.sem, t_xs.at(m, 6))
                    gp.wait_ge(t_dec.sem, t_dec.at(m, 1))
                    for it in range(8):
                        c, g = it // GROUPS, it % GROUPS
                        if it >= 2:
                            gp.wait_ge(t_y.sem, t_y.at(m, it - 1))
                        for d in range(2):
                            h0 = d * HEADS + g * HPG
                            last = G.tensor_tensor(xdt[:, it % 2, d, :].rearrange("p (h d) -> p h d", h=HPG),
                                                   xs[:, c, g * GW:(g + 1) * GW].rearrange("p (h d) -> p h d", h=HPG),
                                                   dtv[:, c, h0:h0 + HPG].unsqueeze(2).to_broadcast([P, HPG, HD]), ALU.mult)
                        last.then_inc(t_xd.sem, 1)
                        gp.wait_ge(t_exp.sem, t_exp.at(m, it + 1))
                        gp.wait_ge(t_sm.sem, t_sm.at(m, it + 1))
                        G.tensor_tensor(seg[:, 1, :, :], seg[:, 1, :, :], smask[:, 1, :].unsqueeze(1).to_broadcast([P, HPG, P]), ALU.mult).then_inc(t_lmB.sem, 1)
                gp.wait_ge(s["sentinel_in"], of(l, "sentinel_in", 16))
                for i in range(nt):
                    gp.wait_ge(s["table_ready"], of(l, "table_ready", i + 1))
                    for j in range(TOPK):
                        gp.indirect_dma_start(scratch["tbl"][l], bass.IndirectOffsetOnAxis(ap=sloti[:, i, j:j + 1], axis=0),
                                              tokid[:, i, j:j + 1], None, bounds_check=P * NB - 1, oob_is_err=False).then_inc(s["table_scattered"], 16)
                gp.wait_ge(s["table_scattered"], of(l, "table_scattered", 16 * nt * TOPK))
                gp.dma_start(tbl[:, 0:NB], scratch["tbl"][l].rearrange("(p b) o -> p (b o)", b=NB)).then_inc(s["table_in"], 16)
                gp.wait_ge(s["table_in"], of(l, "table_in", 16))
                for b in range(2):
                    gp.dma_start(first[:, b:b + 1], scratch["tbl"][l][0:P, :]).then_inc(e_s[l][b], 16)
                gp.wait_ge(s["blocks_ready"], of(l, "blocks_ready", 1))
                gp.wait_ge(s["u2_stored"], of(l, "u2_stored", 16 * nt))
                n = gp.value_load(bexp[0:1, P:P + 1], min_val=1, max_val=NB)
                gp.wait_ge(s_shift[l], 1)

                last_token = gp.to_reg(nt * P - 1)
                last_row = gp.to_reg(nt * P * TOPK - 1)

                def gather(i, b3, b6):
                    G.tensor_copy(idg[:, b6:b6 + 1], tblg[:, bass.ds(i, 1)]).then_inc(s_idg[l], 1)
                    gp.wait_ge(z["xt_tp"], i + 1)
                    gp.wait_ge(s_idg[l], i + 1)
                    gp.sem_inc(s_passed, 1)
                    gp.indirect_dma_start(xg[b3], None, scratch["u2"][l], bass.IndirectOffsetOnAxis(ap=idg[:, b6:b6 + 1], axis=0),
                                          bounds_check=last_token, oob_is_err=False).then_inc(e_g[l][b3], 16)

                for i in range(3):
                    gather(i, i, i)
                with gp.Fori(0, NB // UNR) as ii:
                    for u in range(UNR):
                        i = ii * UNR + u
                        with gp.If(n > i + 3):
                            gather(i + 3, u % 3, (u + 3) % UNR)
                        with gp.If(n > i):
                            G.tensor_copy(ids[:, u:u + 1], tbl[:, bass.ds(i, 1)]).then_inc(s_ids[l], 1)
                            gp.wait_ge(s_ids[l], i + 1)
                            gp.wait_ge(z["y_act"], i + 2)
                            gp.wait_ge(z["y_dve"], i + 2)
                            gp.sem_inc(s_passed, 1)
                            gp.indirect_dma_start(scratch["y"][l], bass.IndirectOffsetOnAxis(ap=ids[:, u:u + 1], axis=0),
                                                  ysb[u % 2], None, bounds_check=last_row, oob_is_err=False).then_inc(e_s[l][u % 2], 16)


_INS = ["x", "c", "ctx", "c_ctx", "w_ada", "b_ada", "w_in", "conv_w", "conv_b", "dt_bias", "a_log", "d_skip",
        "ssm_norm_w", "w_br_ssm", "w_br_four", "w_out", "ln1_g", "ln1_b", "ln2_g", "ln2_b",
        "router_w", "router_bias", "w1", "w3", "w2", "ws1", "ws3", "ws2"]


def kernel(**inputs):
    import numpy as _np
    import concourse.bacc as _bacc
    from concourse import mybir as _mybir
    from concourse.bass_utils import run_bass_kernel_spmd as _run

    nc = _bacc.Bacc("TRN2", target_bir_lowering=False, num_devices=1)
    arrays, ins = {}, {}

    def dram(name, a):
        arrays[name] = a
        return nc.dram_tensor(name, a.shape, _mybir.dt.from_np(a.dtype), kind="ExternalInput").ap()

    for name in _INS:
        a = _np.ascontiguousarray(inputs[name])
        if name == "dt_bias" or name == "a_log":
            a = a.reshape(DEPTH, 2, HEADS)
        ins[name] = dram("in_" + name, a)
    pack, dfts, grid = host_constants()
    consts, dfts, grid = dram("const_pack", pack), dram("const_dft", dfts), dram("const_grid", grid)
    out = nc.dram_tensor("out_0", (1, SEQ, D), F32, kind="ExternalOutput").ap()
    scratch = {
        "u2": [nc.dram_tensor(f"tokens{l}", (len(MOE_TILES[l]) * P, D), F32, kind="Internal").ap() for l in range(DEPTH)],
        "y": [nc.dram_tensor(f"results{l}", (len(MOE_TILES[l]) * P * TOPK, D), F32, kind="Internal").ap() for l in range(DEPTH)],
        "tbl": [nc.dram_tensor(f"slots{l}", (P * NB, 1), I32, kind="Internal").ap() for l in range(DEPTH)],
    }
    hybrid_block_kernel(nc, ins, consts, dfts, grid, out, scratch)
    r = _run(nc, [arrays], core_ids=[0])
    return r.results[0]["out_0"]
```

```python
import concourse.bass as bass
from concourse import mybir
import numpy as np
from contextlib import ExitStack

F32 = mybir.dt.float32
I32 = mybir.dt.int32
ACT = mybir.ActivationFunctionType
ALU = mybir.AluOpType
AX = mybir.AxisListType

P = 128
D = 1024
KD = D // P
SEQ = 256
NT = SEQ // P
DEPTH = 2
HEADS, HD, GROUPS, STATE, CONVW = 24, 64, 4, 128, 5
HPG = HEADS // GROUPS
GW = HPG * HD
DIN = HEADS * HD
CONVCH = DIN + 2 * GROUPS * STATE
OFF_XBC = DIN
OFF_DT = OFF_XBC + CONVCH
OFF_FOUR = OFF_DT + 2 * HEADS
OFF_GATE = OFF_FOUR + D
XT_TILES = DIN // P
CH_TILES = CONVCH // P
FG, FD = 4, 256
NE, FF, TOPK, NGRP, TOPG = 64, 256, 8, 8, 4
EPG = NE // NGRP
NB = 96
SENTINEL = 1 << 20
EPS = 1e-6
ALPHA = (2 * DEPTH) ** 0.25
SW = 256
NSLOT = 4
MSLOT = 3
UNR = 6

C_ID, C_LE, C_GE, C_LT, C_ONE = 0, 128, 256, 384, 512
C_P = 640
C_RANK = 641
C_TOK = C_RANK + TOPK * NE
C_TRI8 = C_TOK + TOPK
NC_COLS = C_TRI8 + NGRP * NGRP


def host_constants():
    p = np.arange(P)
    pack = np.zeros((P, NC_COLS), np.float32)
    pack[:, C_ID:C_ID + P] = np.eye(P)
    pack[:, C_LE:C_LE + P] = p[:, None] <= p[None]
    pack[:, C_GE:C_GE + P] = p[:, None] >= p[None]
    pack[:, C_LT:C_LT + P] = p[:, None] < p[None]
    pack[:, C_ONE:C_ONE + P] = 1.0
    pack[:, C_P] = p
    pack[:, C_RANK:C_RANK + TOPK * NE] = np.repeat(np.arange(TOPK), NE)[None]
    pack[:, C_TOK:C_TOK + TOPK] = p[:, None] * TOPK + np.arange(TOPK)
    g = np.arange(NGRP)
    pack[:, C_TRI8:C_TRI8 + NGRP * NGRP] = (g[None] < g[:, None]).reshape(1, -1)
    n = np.arange(SEQ)
    ang = 2 * np.pi * ((n[:, None] * n[None]) % SEQ) / SEQ
    dft = np.zeros((2, SEQ, 2 * SEQ), np.float32)
    dft[0] = np.concatenate([np.cos(ang), np.sin(ang)], 1)
    dft[1] = np.concatenate([np.cos(ang), -np.sin(ang)], 1) / SEQ
    quarter = D // 4
    omega = (np.float32(1.0) / (np.float32(10000.0) ** (np.arange(quarter, dtype=np.float32) / np.float32(quarter)))).astype(np.float32)
    grid_w = 64
    rows = SEQ // grid_w
    def emb(k):
        a = (np.arange(k, dtype=np.float32)[:, None] * omega).astype(np.float32)
        return np.concatenate([np.sin(a), np.cos(a)], -1)
    er, ec = emb(rows), emb(grid_w)
    pos = np.concatenate([np.broadcast_to(er[:, None], (rows, grid_w, D // 2)),
                          np.broadcast_to(ec[None], (rows, grid_w, D // 2))], -1)
    return pack, dft, np.ascontiguousarray(pos.reshape(SEQ, D).astype(np.float32))


CALLS = [(0, 1, True), (0, 0, True), (1, 1, False), (1, 0, True)]
TILES = {0: [0, 1], 1: [2, 3]}
MOE_TILES = {0: [2, 3, 0, 1], 1: [0, 1]}


def slabs_of(full):
    out = []
    if full:
        out += [("four", j) for j in range(4)]
    out += [("dt", 0)]
    out += [("xbc", j) for j in range(10 if full else 8)]
    if full:
        out += [("z", j) for j in range(6)]
        for j in range(4):
            out += [("g2", j), ("bf", j)]
        out += [("g1", j) for j in range(4)]
        for j in range(4):
            out += [("bsa", j), ("bsb", j)]
        out += [("wo", j) for j in range(4)]
    return out


SLABS = [(m, kind, j) for m, (_, _, full) in enumerate(CALLS) for kind, j in slabs_of(full)]
SLAB_NO = {s: n for n, s in enumerate(SLABS)}
BANK_NO, READER = {}, []
for s in SLABS:
    if s[1] == "bsb":
        BANK_NO[s] = BANK_NO[(s[0], "bsa", s[2])]
    else:
        BANK_NO[s] = len(READER)
        READER.append("act" if s[1] in ("four", "z", "g1", "g2") else "dve")


def freed(bank_no):
    who = READER[bank_no]
    return who, sum(r == who for r in READER[:bank_no + 1])


class Stage:
    def __init__(self, sem, counts):
        self.sem, self.counts = sem, counts

    def at(self, m, k):
        assert 0 < k <= self.counts[m]
        return sum(self.counts[:m]) + k

    def all(self, m):
        return sum(self.counts[:m + 1])


def hybrid_block_kernel(nc, ins, consts, dfts, grid, out, scratch):
    ctx = ExitStack()
    with ctx:
        def sb(name, shape, dt=F32):
            return ctx.enter_context(nc.sbuf_tensor(name, shape, dt))

        def sem(name):
            return ctx.enter_context(nc.semaphore(name))

        def stage(name, full, part=0):
            return Stage(sem(name), [full if f else part for _, _, f in CALLS])

        xres = sb("xres", [P, 4, D])
        cst = sb("cst", [P, NC_COLS])
        ident, tri_le, tri_ge, tri_lt, ones = (cst[:, o:o + P] for o in (C_ID, C_LE, C_GE, C_LT, C_ONE))
        dft = sb("dft", [P, 2, NT, 2 * SEQ])
        modc = sb("modc", [P, 48, 2])
        csil = sb("csil", [P, KD, 2])
        craw = sb("craw", [P, 2, KD])
        lnrow = sb("lnrow", [P, 2, D])
        grow = sb("grow", [P, 2, D])
        par = sb("par", [P, 180])
        praw = sb("praw", [120, 2, P])
        hpar = sb("hpar", [P, 120])
        aneg = sb("aneg", [P, 48])
        stat = sb("stat", [P, 2, 6])
        mv = sb("mv", [P, 2])
        rsq = sb("rsq", [P, 4])
        rsqi = sb("rsqi", [P, 2], I32)
        arena = sb("arena", [P, 39600])
        used = [0]

        def carve(n, at=None):
            o = used[0] if at is None else at
            if at is None:
                used[0] += n
            assert o + n <= 39600, (o, n)
            return arena[:, o:o + n]

        ring = [carve(KD * SW).rearrange("p (k n) -> p k n", n=SW) for _ in range(NSLOT)]
        uT = carve(KD * SEQ).rearrange("p (k t) -> p k t", k=KD)
        mT = carve(KD * SEQ).rearrange("p (k t) -> p k t", k=KD)
        xs_at = used[0]
        xs = carve(NT * DIN).rearrange("p (c n) -> p c n", c=NT)
        ynT = carve(XT_TILES * SEQ, xs_at).rearrange("p (k t) -> p k t", k=XT_TILES)
        zs = carve(NT * DIN).rearrange("p (c n) -> p c n", c=NT)
        btok = carve(NT * GROUPS * STATE).rearrange("p (c n) -> p c n", c=NT)
        bT = carve(GROUPS * SEQ).rearrange("p (g t) -> p g t", g=GROUPS)
        cT = carve(GROUPS * SEQ).rearrange("p (g t) -> p g t", g=GROUPS)
        st = [[carve(DIN).rearrange("p (h d) -> p h d", h=HEADS) for _ in range(2)] for _ in range(2)]
        seg_at = used[0]
        seg = carve(2 * HPG * P).rearrange("p (d h l) -> p d h l", d=2, h=HPG)
        smask = carve(2 * P).rearrange("p (d l) -> p d l", d=2)
        ytmp = carve(3 * GW).rearrange("p (b n) -> p b n", b=3)
        fA = carve(2 * NT * 2 * FD, seg_at).rearrange("p (b t n) -> p b t n", b=2, t=NT)
        lnx_at = used[0]
        xdt = carve(2 * 2 * GW).rearrange("p (b d n) -> p b d n", b=2, d=2)
        wst = carve(2 * GW).rearrange("p (b n) -> p b n", b=2)
        lnx = carve(2 * D, lnx_at).rearrange("p (b n) -> p b n", b=2)
        cacc = grow[:, 1, :].rearrange("p (b t) -> p b t", b=4)
        cxt = carve(4 * SEQ).rearrange("p (b t) -> p b t", b=4)
        fT = carve(KD * SEQ).rearrange("p (k t) -> p k t", k=KD)
        fO = carve(KD * SEQ).rearrange("p (k t) -> p k t", k=KD)
        gT = fT
        dtv = carve(NT * 48).rearrange("p (c n) -> p c n", c=NT)
        adt = carve(NT * 48).rearrange("p (c n) -> p c n", c=NT)
        acu = carve(NT * 96).rearrange("p (c n) -> p c n", c=NT)
        eac = carve(NT * 48).rearrange("p (c n) -> p c n", c=NT)
        dec = carve(NT * 48).rearrange("p (c n) -> p c n", c=NT)
        ecd = carve(NT * 48).rearrange("p (c n) -> p c n", c=NT)
        sp = [carve(NT * 48).rearrange("p (c n) -> p c n", c=NT) for _ in range(4)]
        yrow = cxt[:, 0:2, :]
        rss = carve(NT * 2).rearrange("p (c n) -> p c n", c=NT)
        mixer_words = used[0]

        used[0] = 0
        ew = [carve(6 * D) for _ in range(MSLOT)]
        w13r = [w[:, 0:4 * D].rearrange("p (a r) -> p a r", a=2) for w in ew]
        w13 = [w[:, 0:4 * D].rearrange("p (a k n) -> p k a n", a=2, k=KD) for w in ew]
        w2s = [w[:, 4 * D:6 * D].rearrange("p (k n) -> p k n", k=2) for w in ew]
        yall = [arena[:, b * TOPK * D:(b + 1) * TOPK * D].rearrange("p (j n) -> p j n", j=TOPK) for b in range(2)]
        modrow = arena[0:2, 2 * TOPK * D:2 * TOPK * D + 6 * D]
        u2T = carve(KD * 4 * P).rearrange("p (k t) -> p k t", k=KD)
        macc = carve(4 * D).rearrange("p (t n) -> p t n", t=4)
        aring = [carve(KD * SW, used[0] + b * KD * SW).rearrange("p (k n) -> p k n", n=SW) for b in range(4)]
        xg = [carve(D) for _ in range(3)]
        xTe = [carve(D).rearrange("p (k t) -> p k t", k=KD) for _ in range(2)]
        hs = [carve(FF) for _ in range(2)]
        hh = [carve(FF) for _ in range(2)]
        hT = [carve(2 * P).rearrange("p (k t) -> p k t", k=2) for _ in range(2)]
        ysb = [carve(D) for _ in range(2)]
        ln2x = carve(2 * D).rearrange("p (b n) -> p b n", b=2)
        rw = carve(KD * NE).rearrange("p (k e) -> p k e", k=KD)
        rbias = carve(NE)
        msk = carve(4 * NE).rearrange("p (t e) -> p t e", t=4)
        gat = carve(4 * TOPK).rearrange("p (t j) -> p t j", t=4)
        rt = [carve(NE) for _ in range(8)]
        scores = [rt[0], carve(NE)]
        r8 = [carve(8) for _ in range(6)]
        cube = carve(TOPK * NE)
        slotf = carve(4 * TOPK).rearrange("p (t j) -> p t j", t=4)
        sloti = sb("sloti", [P, 4, TOPK], I32)
        tokid = sb("tokid", [P, 4, TOPK], I32)
        tbl = sb("tbl", [P, NB + UNR], I32)
        tblg = sb("tblg", [P, NB + UNR], I32)
        idg = sb("idg", [P, UNR], I32)
        ids = sb("ids", [P, UNR], I32)
        sent = sb("sent", [P, NB], I32)
        bexp = sb("bexp", [1, P + 2], I32)
        ecol = sb("ecol", [P, 1])
        first = sb("first", [P, 2], I32)

        psum = ctx.enter_context(nc.psum_tensor("psum", [P, 8, 512], F32))
        bank = [psum[:, i, :] for i in range(8)]

        s_const = sem("constants_in")
        s_x = sem("x_in")
        s_c = sem("c_in")
        s_csil = sem("csil_ready")
        s_xin = sem("x_plus_pos")
        s_par = sem("params_in")
        s_tp_par = sem("params_transposed")
        s_parc = sem("params_ready")
        s_lnrow = sem("lnrow_in")
        s_lnrow_free = sem("lnrow_used")
        s_ada = [sem(f"ada_in{i}") for i in range(4)]
        s_ada_mm = sem("ada_product")
        s_ada_row = sem("ada_row")
        s_ada_tp = sem("ada_transposed")
        s_modc = sem("modulation_ready")
        s_slab_in = [sem(f"slab_in{i}") for i in range(NSLOT)]
        s_slab = sem("slab_product")
        s_read = {"act": sem("act_read_product"), "dve": sem("dve_read_product")}
        s_chain = sem("dve_chain")
        s_achain = sem("act_chain")
        s_pchain = sem("pool_chain")
        t_lnx = stage("u_normed", 2, 2)
        t_utp = stage("u_transposed", 2, 2)
        t_uT = stage("u_ready", 2, 2)
        t_acc = stage("conv_first_tap", 10, 8)
        t_cv = stage("conv_done", 10, 8)
        t_cs = stage("conv_silu", 10, 8)
        t_ctp = stage("conv_transposed", 8, 8)
        t_xs = stage("conv_token_major", 8, 8)
        t_dtx = stage("dt_exp", 1, 1)
        t_dtr = stage("dt_raw", 1, 1)
        t_adt = stage("adt_ready", 1, 1)
        t_acp = stage("cumulated_product", 1, 1)
        t_acu = stage("cumulated_ready", 1, 1)
        t_eac = stage("exp_cumulated", 1, 1)
        t_dec = stage("decay_ready", 1, 1)
        t_w = Stage(sem("weighted_x_ready"), [16 if c[1] else 8 for c in CALLS])
        t_stp = Stage(sem("state_product"), [16 if c[1] else 8 for c in CALLS])
        t_st = Stage(sem("state_ready"), [16 if c[1] else 8 for c in CALLS])
        t_f1 = stage("dft_feature_product", 4, 0)
        t_f1c = stage("dft_feature_ready", 4, 0)
        t_f2 = stage("dft_token_product", 4, 0)
        t_f2c = stage("dft_token_ready", 4, 0)
        t_row = stage("cumulated_rows", 16, 0)
        t_rowr = stage("cumulated_rows_read", 16, 0)
        t_seg = stage("segments_ready", 8, 0)
        t_exp = stage("decay_matrix", 8, 0)
        t_sm = stage("masked_scores", 8, 0)
        t_lmF = stage("weighted_scores_forward", 8, 0)
        t_lmB = stage("weighted_scores_backward", 8, 0)
        t_xd = stage("x_dt_ready", 8, 0)
        t_y = stage("y_products", 8, 0)
        t_yr = stage("y_products_read", 8, 0)
        t_h = stage("gated_y", 2, 0)
        t_ss = stage("square_sum", 2, 0)
        t_yn = stage("normed_y", 2, 0)
        t_ytp = stage("y_transposed", 6, 0)
        t_yT = stage("y_channel_major", 6, 0)
        t_mT2 = stage("fourier_merged", 4, 0)
        t_mT = stage("merged", 4, 0)
        t_gd = stage("gate_diagonals", 8, 0)
        t_gp = stage("gate_rows_product", 1, 0)
        t_gr = stage("gate_rows_ready", 1, 0)

        names = ("u2_normed u2_transposed u2_ready logits routed counted placed rank_tp blocks_ready "
                 "back_tp back_copied u2_stored0 u2_stored1 sentinel_in table_scattered table_in table_ready "
                 "router_in shared_in shared_up shared_sil shared_h shared_ht shared_htc shared_y shared_out "
                 "g2_diag g2_rows g2_ready scores").split()
        s = {n: sem(n) for n in names}
        nt0 = len(MOE_TILES[0])
        fixed = {"counted": 1, "placed": 1, "rank_tp": 1, "blocks_ready": 1, "u2_stored0": 8 * nt0, "u2_stored1": 8 * nt0, "sentinel_in": 16,
                 "table_scattered": 16 * nt0 * TOPK, "table_in": 16, "router_in": 32, "shared_in": 48,
                 "g2_diag": KD * nt0 // 2, "g2_rows": nt0 // 2, "g2_ready": nt0 // 2}

        def of(l, name, k):
            return k + (fixed.get(name, nt0) if l else 0)

        e_names = "xt_tp xt_act xt_dve up silu h_ready ht_tp ht_copied down y_act y_dve".split()
        e = [{n: sem(f"e_{n}{l}") for n in e_names} for l in range(DEPTH)]
        e_w = [[sem(f"e_w{l}{i}") for i in range(MSLOT)] for l in range(DEPTH)]
        e_w2 = [[sem(f"e_w2{l}{i}") for i in range(MSLOT)] for l in range(DEPTH)]
        e_g = [[sem(f"e_g{l}{i}") for i in range(3)] for l in range(DEPTH)]
        e_s = [[sem(f"e_s{l}{i}") for i in range(2)] for l in range(DEPTH)]
        e_yin = [sem(f"e_yin{b}") for b in range(2)]
        e_comb = [sem(f"e_comb{l}") for l in range(DEPTH)]
        s_shift = [sem(f"token_table{l}") for l in range(DEPTH)]
        s_idg = [sem(f"gather_index{l}") for l in range(DEPTH)]
        s_ids = [sem(f"scatter_index{l}") for l in range(DEPTH)]
        s_passed = sem("pool_passed")
        e_done = sem("blocks_done")
        s_out = sem("out_stored")

        block = ctx.enter_context(nc.Block())

        def ada_cols(i):
            return bass.ds(i * SW, SW)

        @block.sync
        def _(sp):
            sp.dma_start(craw[:, 0, :], ins["c"][0].rearrange("(p k) -> p k", k=KD)).then_inc(s_c, 16)
            sp.dma_start(craw[:, 1, :], ins["c_ctx"].rearrange("(p k) -> p k", k=KD)).then_inc(s_c, 16)
            sp.dma_start(cst[:, :], consts).then_inc(s_const, 16)

            def streams():
                for t in range(NT):
                    sp.dma_start(xres[:, t, :], ins["x"][0, t * P:(t + 1) * P, :]).then_inc(s_x, 16)
                    sp.dma_start(xres[:, NT + t, :], ins["ctx"][0, t * P:(t + 1) * P, :]).then_inc(s_x, 16)
                    sp.dma_start(ring[0].rearrange("p k n -> p (k n)")[:, t * D:(t + 1) * D], grid[t * P:(t + 1) * P, :]).then_inc(s_x, 16)
                for a in range(2):
                    sp.dma_start(dft[:, a, :, :], dfts[a].rearrange("(t p) n -> p t n", p=P)).then_inc(s_x, 16)

            def params(l):
                if l:
                    sp.wait_ge(s_parc, 2 * l)
                    sp.wait_ge(t_yT.sem, t_yT.all(1))
                    sp.wait_ge(t_yn.sem, t_yn.all(1))
                sp.dma_start(praw[0:48, 0, :], ins["b_ada"][l].rearrange("(j p) -> j p", p=P)).then_inc(s_par, 16)
                sp.dma_start(praw[48:60, 0, :], ins["ssm_norm_w"][l].rearrange("(j p) -> j p", p=P)).then_inc(s_par, 16)
                sp.dma_start(praw[0:100, 1, :], ins["conv_w"][l].rearrange("t (j p) -> (t j) p", p=P)).then_inc(s_par, 16)
                sp.dma_start(praw[100:120, 1, :], ins["conv_b"][l].rearrange("(j p) -> j p", p=P)).then_inc(s_par, 16)
                hp = [(0, 48, ins["dt_bias"][l:l + 1].rearrange("a d h -> a (d h)")),
                      (48, 48, ins["a_log"][l:l + 1].rearrange("a d h -> a (d h)")),
                      (96, 24, ins["d_skip"][l:l + 1, :])]
                for o, n, src in hp:
                    sp.dma_start(hpar[:, o:o + n], src.to_broadcast([P, n])).then_inc(s_par, 16)

            def modulation(l):
                wsrc = ins["w_ada"][l].rearrange("(p k) n -> p k n", k=KD)
                with sp.Fori(0, 6) as i:
                    for b in range(4):
                        sp.wait_ge(s_ada_mm, (i * 4 + b + 1) + 28 * l)
                        sp.dma_start(aring[b][:, :, :], wsrc[:, :, ada_cols(i * 4 + b)]).then_inc(s_ada[b], 16)

            def slab(m, kind, j):
                l = CALLS[m][0]
                n = SLAB_NO[(m, kind, j)]
                if n >= NSLOT:
                    sp.wait_ge(s_slab, n - NSLOT + 1)
                slot, w = ring[n % NSLOT], ins["w_in"][l]
                if kind in ("bsa", "bsb"):
                    k0 = 6 if kind == "bsb" else 0
                    src = ins["w_br_ssm"][l].rearrange("(k p) n -> p k n", p=P)[:, k0:k0 + 6, j * SW:(j + 1) * SW]
                    sp.dma_start(slot[:, 0:6, :], src).then_inc(s_slab_in[n % NSLOT], 16)
                    return
                c0, cn = {"four": (OFF_FOUR, SW), "xbc": (OFF_XBC, SW), "z": (0, SW), "dt": (OFF_DT, 48),
                          "g1": (OFF_GATE, SW), "g2": (OFF_GATE + D, SW)}.get(kind, (0, SW))
                if kind == "bf":
                    w = ins["w_br_four"][l]
                if kind == "wo":
                    w = ins["w_out"][l]
                src = w.rearrange("(k p) n -> p k n", p=P)[:, :, c0 + j * cn:c0 + (j + 1) * cn]
                sp.dma_start(slot[:, :, 0:cn], src).then_inc(s_slab_in[n % NSLOT], 16)

            def post_norm_rows(l, g, b, which):
                if which:
                    sp.wait_ge(s_lnrow_free, which)
                sp.dma_start(lnrow[:, 0, :], ins[g][l:l + 1, :].to_broadcast([P, D])).then_inc(s_lnrow, 16)
                sp.dma_start(lnrow[:, 1, :], ins[b][l:l + 1, :].to_broadcast([P, D])).then_inc(s_lnrow, 16)

            norm = 0
            for l in range(DEPTH):
                params(l)
                modulation(l)
                if l == 0:
                    streams()
                sp.wait_ge(s_xin, 1)
                if l:
                    sp.wait_ge(e_comb[l - 1], len(MOE_TILES[l - 1]))
                for m, (cl, _, full) in enumerate(CALLS):
                    if cl == l:
                        for n_, (kind, j) in enumerate(slabs_of(full)):
                            slab(m, kind, j)
                            if full and n_ == NSLOT:
                                post_norm_rows(l, "ln1_g", "ln1_b", norm)
                                norm += 1
                nt = len(MOE_TILES[l])
                m = 2 * l + 1
                sp.wait_ge(t_mT.sem, t_mT.all(m))
                sp.wait_ge(s_slab, SLAB_NO[(m, "wo", 3)] + 1)
                sp.wait_ge(s_read["dve"], freed(BANK_NO[(m, "wo", 3)])[1])
                sp.dma_start(rw[:, :, :], ins["router_w"][l].rearrange("(k p) n -> p k n", p=P)).then_inc(s["router_in"], 16)
                sp.dma_start(rbias[:, :], ins["router_bias"][l:l + 1, :].to_broadcast([P, NE])).then_inc(s["router_in"], 16)
                sp.dma_start(w13r[2][:, 0, :].rearrange("p (k n) -> p k n", k=KD), ins["ws1"][l].rearrange("(k p) n -> p k n", p=P)).then_inc(s["shared_in"], 16)
                sp.dma_start(w13r[2][:, 1, :].rearrange("p (k n) -> p k n", k=KD), ins["ws3"][l].rearrange("(k p) n -> p k n", p=P)).then_inc(s["shared_in"], 16)
                sp.dma_start(ew[2][:, 4 * D:6 * D], ins["ws2"][l].rearrange("(p k) n -> p (k n)", p=P)).then_inc(s["shared_in"], 16)
                post_norm_rows(l, "ln2_g", "ln2_b", norm)
                norm += 1
                for i, t in enumerate(MOE_TILES[l]):
                    sp.wait_ge(s["back_copied"], of(l, "back_copied", i + 1))
                    sp.dma_start(scratch["u2"][l][i * P:(i + 1) * P, :], macc[:, i, :]).then_inc(s[f"u2_stored{i % 2}"], 16)
                sp.wait_ge(s["blocks_ready"], of(l, "blocks_ready", 1))
                n = sp.value_load(bexp[0:1, P:P + 1], min_val=1, max_val=NB)

                def expert_of(i):
                    return sp.value_load(bexp[0:1, bass.ds(i, 1)], min_val=0, max_val=NE - 1)

                def up_in(i, b):
                    ex = expert_of(i)
                    for a, src in ((0, "w1"), (1, "w3")):
                        sp.dma_start(w13r[b][:, a, :], ins[src][l, bass.ds(ex, 1), :, :].rearrange("a (p k) n -> p (a k n)", p=P)).then_inc(e_w[l][b], 16)

                def down_in(i, b):
                    ex = expert_of(i)
                    sp.dma_start(ew[b][:, 4 * D:6 * D], ins["w2"][l, bass.ds(ex, 1), :, :].rearrange("a (p k) n -> p (a k n)", p=P)).then_inc(e_w2[l][b], 16)

                for i in range(2):
                    up_in(i, i)
                    down_in(i, i)
                sp.wait_ge(s["shared_y"], of(l, "shared_y", nt))
                up_in(2, 2)
                with sp.Fori(0, NB // UNR) as ii:
                    with sp.If(n > ii * UNR):
                        for u in range(UNR):
                            i = ii * UNR + (u + 2)
                            with sp.If(n > i + 1):
                                sp.wait_ge(e[l]["up"], i + 1)
                                up_in(i + 1, u % MSLOT)
                            with sp.If(n > i):
                                sp.wait_ge(e[l]["down"], i + 1)
                                down_in(i, (u + 2) % MSLOT)
                if l == 0:
                    sp.wait_ge(e_done, 1)
            for i in range(NT):
                sp.wait_ge(e_comb[1], i + 1)
                sp.dma_start(out[0, i * P:(i + 1) * P, :], xres[:, i, :]).then_inc(s_out, 16)
            sp.wait_ge(s_out, 16 * NT)

        @block.tensor
        def _(pe):
            mm = nc.tensor.matmul
            tp = nc.tensor.transpose
            pe.sem_inc(s_ada_mm, 4)
            pe.wait_ge(s_const, 16)
            for l in range(DEPTH):
                pe.wait_ge(s_par, 16 * 7 * (l + 1))
                tp(bank[7][:, 0:60], praw[0:60, 0, :], ident[0:60, 0:60])
                tp(bank[7][:, 60:180], praw[0:120, 1, :], ident[0:120, 0:120]).then_inc(s_tp_par, 1)
                pe.wait_ge(s_csil, 1)
                with pe.Fori(0, 6) as i:
                    for b in range(4):
                        pe.wait_ge(s_ada_row, i * 4 + b + 1 + 24 * l)
                        pe.wait_ge(s_ada[b], (i + 1) * 16 + 96 * l)
                        for k in range(KD):
                            last = mm(bank[b % 2][0:2, 0:SW], csil[:, k, :], aring[b][:, k, :], start=k == 0, stop=k == KD - 1)
                        last.then_inc(s_ada_mm, 1)
                pe.wait_ge(s_ada_row, 24 * (l + 1) + 2)
                for c in range(48):
                    last = tp(bank[3][:, 2 * c:2 * c + 2], modrow[:, c * P:(c + 1) * P], ident[0:2, 0:2])
                last.then_inc(s_ada_tp, 1)
                pe.sem_inc(s_ada_mm, 4)

                for m, (cl, stream, full) in enumerate(CALLS):
                    if cl != l:
                        continue
                    for t in range(NT):
                        pe.wait_ge(t_lnx.sem, t_lnx.at(m, t + 1))
                        if t == 0:
                            pe.wait_ge(s_modc, l + 1)
                        for k in range(KD):
                            last = tp(psum[:, 3 + 2 * t + k // 4, (k % 4) * P:(k % 4 + 1) * P], lnx[:, t, k * P:(k + 1) * P], ident)
                        last.then_inc(t_utp.sem, 1)
                    pe.wait_ge(t_uT.sem, t_uT.at(m, 2))

                    def begin(kind, j):
                        n = SLAB_NO[(m, kind, j)]
                        b = BANK_NO[(m, kind, j)]
                        pe.wait_ge(s_slab_in[n % NSLOT], 16 * (n // NSLOT + 1))
                        if b >= 2 and kind != "bsb":
                            who, cnt = freed(b - 2)
                            pe.wait_ge(s_read[who], cnt)
                        return ring[n % NSLOT], bank[b % 2].rearrange("p (a t) -> p a t", a=2)

                    def channel_major(kind, j, rhs, ks, first=True, final=True):
                        w, o = begin(kind, j)
                        for a in range(2):
                            for k in range(ks):
                                last = mm(o[:, a, :], w[:, k, a * P:(a + 1) * P], rhs[:, k, :],
                                          start=first and k == 0, stop=final and k == ks - 1, skip_group_check=True)
                        last.then_inc(s_slab, 1)

                    def token_major(kind, j, lhs, cols):
                        w, o = begin(kind, j)
                        for a in range(NT):
                            for k in range(KD):
                                last = mm(o[:, a, 0:cols], lhs[:, k, a * P:(a + 1) * P], w[:, k, 0:cols], start=k == 0, stop=k == KD - 1)
                        last.then_inc(s_slab, 1)

                    def conv_transpose(j):
                        pe.wait_ge(t_cs.sem, t_cs.at(m, j + 1))
                        if j >= 2:
                            pe.wait_ge(t_xs.sem, t_xs.at(m, j - 1))
                        o = bank[2 + 5 * (j % 2)]
                        for a in range(2):
                            ch = 2 * j + a
                            src = cxt[:, (2 * j + a) % 4, :] if ch < XT_TILES else bT[:, ch - XT_TILES, :]
                            for c in range(NT):
                                last = tp(o[:, c * SW + a * P:c * SW + (a + 1) * P], src[:, c * P:(c + 1) * P], ident)
                        last.then_inc(t_ctp.sem, 1)

                    if full:
                        for j in range(4):
                            channel_major("four", j, uT, KD)
                    token_major("dt", 0, uT, 48)
                    for j in range(10 if full else 8):
                        channel_major("xbc", j, uT, KD)
                        if 2 <= j < 10:
                            conv_transpose(j - 2)
                    if not full:
                        conv_transpose(6)
                        conv_transpose(7)
                    pe.wait_ge(t_adt.sem, t_adt.at(m, 1))
                    for c in range(NT):
                        mm(bank[5][:, c * 96:c * 96 + 24], tri_le, adt[:, c, 0:24], start=True, stop=True)
                        mm(bank[5][:, c * 96 + 24:c * 96 + 48], tri_ge, adt[:, c, 24:48], start=True, stop=True)
                        last = mm(bank[5][:, c * 96 + 48:c * 96 + 96], ones, adt[:, c, :], start=True, stop=True)
                    last.then_inc(t_acp.sem, 1)
                    if full:
                        for j in range(6):
                            token_major("z", j, uT, SW)

                        def feature_dft(g):
                            if g >= 1:
                                pe.wait_ge(t_f1c.sem, t_f1c.at(m, g))
                            for t in range(NT):
                                for k in range(2):
                                    last = mm(bank[3 + t][:, :], fT[:, 2 * g + k, t * P:(t + 1) * P], dft[:, 0, k, :], start=k == 0, stop=k == 1)
                            last.then_inc(t_f1.sem, 1)

                        def token_dft(g):
                            pe.wait_ge(t_f1c.sem, t_f1c.at(m, g + 1))
                            if g >= 1:
                                pe.wait_ge(t_f2c.sem, t_f2c.at(m, g))
                            for a in range(2):
                                for i, (t, part) in enumerate([(t, part) for t in range(NT) for part in range(2)]):
                                    last = mm(bank[6][:, a * SEQ:(a + 1) * SEQ],
                                              fA[:, g % 2, t, part * FD + a * P:part * FD + (a + 1) * P],
                                              dft[:, 1, t, part * SEQ:(part + 1) * SEQ], start=i == 0, stop=i == 3)
                            last.then_inc(t_f2.sem, 1)

                        for g in range(GROUPS):
                            feature_dft(g)
                            if g:
                                token_dft(g - 1)
                        token_dft(GROUPS - 1)

                    def state_product(i, c, g):
                        pe.wait_ge(t_w.sem, t_w.at(m, i + 1))
                        if i == 0:
                            pe.wait_ge(t_acu.sem, t_acu.at(m, 1))
                        if i == 0 and full:
                            pe.wait_ge(t_f2c.sem, t_f2c.at(m, 4))
                        if i >= 2:
                            pe.wait_ge(t_st.sem, t_st.at(m, i - 1))
                        mm(bank[5 + i % 2][:, 0:GW], btok[:, c, g * STATE:(g + 1) * STATE], wst[:, i % 2, :], start=True, stop=True).then_inc(t_stp.sem, 1)

                    pe.wait_ge(t_xs.sem, t_xs.at(m, 8))
                    for i, (c, g) in enumerate([(0, g) for g in range(4)] + [(1, g) for g in range(4)]):
                        state_product(i, c, g)

                    if full:
                        def rows(it):
                            c, g = it // GROUPS, it % GROUPS
                            for d in range(2):
                                if it or d:
                                    pe.wait_ge(t_rowr.sem, t_rowr.at(m, 2 * it + d))
                                if d == 0:
                                    if it:
                                        pe.wait_ge(t_sm.sem, t_sm.at(m, it))
                                    mm(bank[4][:, 256:384], bT[:, g, c * P:(c + 1) * P], cT[:, g, c * P:(c + 1) * P], start=True, stop=True)
                                tri = tri_le if d == 0 else tri_ge
                                for r in range(HPG):
                                    h = d * HEADS + g * HPG + r
                                    last = mm(psum[:, 3 + r // 4, (r % 4) * P:(r % 4 + 1) * P],
                                              adt[:, c, h:h + 1].to_broadcast([P, P]), tri, start=True, stop=True)
                                last.then_inc(t_row.sem, 1)

                        def y_products(it):
                            c, g = it // GROUPS, it % GROUPS
                            pe.wait_ge(t_lmF.sem, t_lmF.at(m, it + 1))
                            pe.wait_ge(t_lmB.sem, t_lmB.at(m, it + 1))
                            pe.wait_ge(t_xd.sem, t_xd.at(m, it + 1))
                            if it:
                                pe.wait_ge(t_yr.sem, t_yr.at(m, it))
                            else:
                                pe.wait_ge(t_st.sem, t_st.at(m, 8))
                            for r in range(HPG):
                                o = bank[5][:, r * HD:(r + 1) * HD]
                                mm(o, seg[:, 0, r, :], xdt[:, it % 2, 0, r * HD:(r + 1) * HD], start=True, stop=False)
                                last = mm(o, seg[:, 1, r, :], xdt[:, it % 2, 1, r * HD:(r + 1) * HD], start=False, stop=True)
                            for d in range(2):
                                which = c if d == 0 else 1 - c
                                if stream == 0 or which == 1:
                                    last = mm(bank[6 + d][:, 0:GW], cT[:, g, c * P:(c + 1) * P],
                                              st[d][which][:, g * HPG:(g + 1) * HPG, :].rearrange("p h d -> p (h d)"), start=True, stop=True)
                            last.then_inc(t_y.sem, 1)

                        for it in range(8):
                            if it == 0:
                                pe.wait_ge(t_cs.sem, t_cs.at(m, 10))
                                pe.wait_ge(t_xs.sem, t_xs.at(m, 8))
                            rows(it)
                            j = it // 2
                            channel_major("g2" if it % 2 == 0 else "bf", j, uT if it % 2 == 0 else fO, KD)
                            y_products(it)

                    if stream == 1:
                        for i, (c, g) in enumerate([(1, g) for g in range(4)] + [(0, g) for g in range(4)]):
                            state_product(8 + i, c, g)

                    if full:
                        for j in range(4):
                            channel_major("g1", j, uT, KD)
                        for c in range(NT):
                            pe.wait_ge(t_yn.sem, t_yn.at(m, c + 1))
                            for b in range(3):
                                k = 3 * c + b
                                if k >= 2:
                                    pe.wait_ge(t_yT.sem, t_yT.at(m, k - 1))
                                for a in range(4):
                                    ch = 4 * b + a
                                    last = tp(bank[2 + 5 * (k % 2)][:, a * P:(a + 1) * P], zs[:, c, ch * P:(ch + 1) * P], ident)
                                last.then_inc(t_ytp.sem, 1)
                        pe.wait_ge(t_yT.sem, t_yT.at(m, 6))
                        for j in range(4):
                            w, o = begin("bsa", j)
                            w2, _ = begin("bsb", j)
                            for a in range(2):
                                for k in range(6):
                                    last = mm(o[:, a, :], w[:, k, a * P:(a + 1) * P], ynT[:, k, :], start=k == 0, stop=False)
                                if a == 1:
                                    last.then_inc(s_slab, 1)
                                for k in range(6):
                                    last = mm(o[:, a, :], w2[:, k, a * P:(a + 1) * P], ynT[:, 6 + k, :], start=False, stop=k == 5)
                            last.then_inc(s_slab, 1)
                        for k in range(KD):
                            pe.wait_ge(t_gd.sem, t_gd.at(m, k + 1))
                            last = mm(psum[:, 3 + k // 4, (k % 4) * P:(k % 4 + 1) * P], ones, lnx[:, 0, k * P:(k + 1) * P], start=True, stop=True)
                        last.then_inc(t_gp.sem, 1)
                        pe.wait_ge(t_mT.sem, t_mT.at(m, 4))
                        for j in range(4):
                            token_major("wo", j, mT, SW)

                z, nt = e[l], len(MOE_TILES[l])
                def u2_products(i):
                    pe.wait_ge(s["u2_normed"], of(l, "u2_normed", i + 1))
                    if i:
                        pe.wait_ge(s["u2_ready"], of(l, "u2_ready", i))
                    for k in range(KD):
                        last = tp(psum[:, 3 + k // 4, (k % 4) * P:(k % 4 + 1) * P], ln2x[:, i % 2, k * P:(k + 1) * P], ident)
                    last.then_inc(s["u2_transposed"], 1)
                    pe.wait_ge(s["u2_ready"], of(l, "u2_ready", i + 1))
                    if i == 0:
                        pe.wait_ge(s["router_in"], of(l, "router_in", 32))
                    else:
                        pe.wait_ge(s["scores"], of(l, "scores", i))
                        pe.wait_ge(s["back_copied"], of(l, "back_copied", i))
                    for k in range(KD):
                        last = mm(bank[2][:, 0:NE], u2T[:, k, i * P:(i + 1) * P], rw[:, k, :], start=k == 0, stop=k == KD - 1)
                    last.then_inc(s["logits"], 1)
                    if i >= 2:
                        pe.wait_ge(s["shared_out"], of(l, "shared_out", i - 1))
                    for k in range(KD):
                        last = tp(psum[:, 5 + k // 4, (k % 4) * P:(k % 4 + 1) * P], u2T[:, k, i * P:(i + 1) * P], ident)
                    last.then_inc(s["back_tp"], 1)

                def up(o, lhs, w, between=None):
                    for k in range(KD):
                        if k == KD // 2 and between:
                            between()
                        last = mm(o.rearrange("p (a n) -> p a n", a=2), lhs(k), w[:, k, :, :], start=k == 0, stop=k == KD - 1)
                    return last

                def h_transpose(src):
                    hk = src.rearrange("p (f k) -> p k f", k=2)
                    tp(bank[4][:, 0:P], hk[:, 0, :], ident)
                    return tp(bank[4][:, P:2 * P], hk[:, 1, :], ident)

                def down(src, w):
                    for half in range(2):
                        for k in range(2):
                            last = mm(bank[5 + half][:, :], src[:, k, :], w[:, k, half * 512:(half + 1) * 512], start=k == 0, stop=k == 1)
                    return last

                u2_products(0)
                pe.wait_ge(s["shared_in"], of(l, "shared_in", 48))
                for i in range(nt):
                    up(bank[i % 2], lambda k: u2T[:, k, i * P:(i + 1) * P], w13[2]).then_inc(s["shared_up"], 1)
                    if i + 1 < nt:
                        u2_products(i + 1)
                    else:
                        pe.wait_ge(s["routed"], of(l, "routed", nt))
                        for c in range(nt):
                            for b in range(c):
                                mm(bank[7][:, c * NE:(c + 1) * NE], ones, msk[:, b, :], start=b == 0, stop=False)
                            mm(bank[7][:, c * NE:(c + 1) * NE], tri_lt, msk[:, c, :], start=c == 0, stop=True)
                        for b in range(nt):
                            last = mm(bank[7][:, 4 * NE:5 * NE], ones, msk[:, b, :], start=b == 0, stop=b == nt - 1)
                        last.then_inc(s["counted"], 1)
                    pe.wait_ge(s["shared_h"], of(l, "shared_h", i + 1))
                    h_transpose(hh[i % 2]).then_inc(s["shared_ht"], 1)
                    pe.wait_ge(s["shared_htc"], of(l, "shared_htc", i + 1))
                    pe.wait_ge(s["back_copied"], of(l, "back_copied", min(i + 2, nt)))
                    if i:
                        pe.wait_ge(s["shared_out"], of(l, "shared_out", i))
                    down(hT[i % 2], w2s[2]).then_inc(s["shared_y"], 1)
                for v in range(nt // 2):
                    for k in range(KD):
                        pe.wait_ge(s["g2_diag"], of(l, "g2_diag", v * KD + k + 1))
                        last = mm(psum[:, 2 + k // 4, (k % 4) * P:(k % 4 + 1) * P], ones, ln2x[:, v, k * P:(k + 1) * P], start=True, stop=True)
                    last.then_inc(s["g2_rows"], 1)
                    pe.wait_ge(s["g2_ready"], of(l, "g2_ready", v + 1))
                pe.wait_ge(s["placed"], of(l, "placed", 1))
                tp(bank[7][0:1, 0:P], ecol[:, 0:1], ident).then_inc(s["rank_tp"], 1)
                pe.wait_ge(s["shared_out"], of(l, "shared_out", nt))
                pe.sem_inc(z["down"], 3)
                pe.sem_inc(z["up"], 2)
                pe.sem_inc(z["xt_tp"], 3)
                pe.sem_inc(z["ht_tp"], 2)
                pe.wait_ge(s["blocks_ready"], of(l, "blocks_ready", 1))
                n = pe.value_load(bexp[0:1, P:P + 1], min_val=1, max_val=NB)

                def x_transpose(i, b3, rounds):
                    pe.wait_ge(e_g[l][b3], rounds * 16)
                    pe.wait_ge(z["xt_act"], i + 1)
                    pe.wait_ge(z["xt_dve"], i + 1)
                    for k in range(KD):
                        last = tp(psum[:, 2 + k // 4, (k % 4) * P:(k % 4 + 1) * P], xg[b3].rearrange("p (q k) -> p k q", k=KD)[:, k, :], ident)
                    last.then_inc(z["xt_tp"], 1)

                def block_up(i, b2, b3, rounds, between=None):
                    pe.wait_ge(z["xt_act"], i + 2)
                    pe.wait_ge(z["xt_dve"], i + 2)
                    pe.wait_ge(e_w[l][b3], rounds * 32)
                    pe.wait_ge(z["h_ready"], i + 1)
                    up(bank[b2], lambda k: xTe[b2][:, k, :], w13[b3], between).then_inc(z["up"], 1)

                def block_ht(i, b2):
                    pe.wait_ge(z["h_ready"], i + 3)
                    pe.wait_ge(z["ht_copied"], i + 1)
                    h_transpose(hh[b2]).then_inc(z["ht_tp"], 1)

                def block_down(i, b2, b3, rounds):
                    pe.wait_ge(e_w2[l][b3], rounds * 16)
                    pe.wait_ge(z["ht_copied"], i + 2)
                    pe.wait_ge(z["y_act"], i + 1)
                    pe.wait_ge(z["y_dve"], i + 1)
                    down(hT[b2], w2s[b3]).then_inc(z["down"], 1)

                x_transpose(0, 0, 1)
                x_transpose(1, 1, 1)
                block_up(0, 0, 0, 1)
                with pe.Fori(0, NB // UNR) as ii:
                    with pe.If(n > ii * UNR):
                        for u in range(UNR):
                            i = ii * UNR + u
                            with pe.If(n > i + 2):
                                x_transpose(i + 2, (u + 2) % 3, ii * 2 + (u + 2) // 3 + 1)
                            with pe.If(n > i + 1):
                                block_up(i + 1, (u + 1) % 2, (u + 1) % 3, ii * 2 + (u + 1) // 3 + 1,
                                         lambda: block_ht(i, u % 2))
                                block_down(i, u % 2, u % 3, ii * 2 + u // 3 + 1)
                            with pe.If(n > i):
                                with pe.If(n < i + 2):
                                    block_ht(i, u % 2)
                                    block_down(i, u % 2, u % 3, ii * 2 + u // 3 + 1)

        @block.scalar
        def _(act):
            a_ = nc.scalar.activation
            count = {"chain": 0, "ln": 0}

            def link(ins_):
                count["chain"] += 1
                ins_.then_inc(s_achain, 1)
                act.wait_ge(s_achain, count["chain"])

            act.wait_ge(s_c, 32)
            for v in range(2):
                last = a_(csil[:, :, v], craw[:, v, :], ACT.Silu)
            last.then_inc(s_csil, 1)
            act.sem_inc(s_ada_row, 2)
            for l in range(DEPTH):
                act.wait_ge(s_tp_par, l + 1)
                a_(par[:, :], bank[7][:, 0:180], ACT.Copy).then_inc(s_parc, 1)
                act.wait_ge(s_par, 16 * 7 * (l + 1))
                link(a_(aneg[:, :], hpar[:, 48:96], ACT.Exp))
                a_(aneg[:, :], aneg[:, :], ACT.Copy, scale=-1.0).then_inc(s_parc, 1)
                with act.Fori(0, 6) as i:
                    for b in range(4):
                        act.wait_ge(s_ada_mm, i * 4 + b + 5 + 28 * l)
                        a_(modrow[:, bass.ds((i * 4 + b) * SW, SW)], bank[b % 2][0:2, 0:SW], ACT.Copy).then_inc(s_ada_row, 1)

                for m, (cl, stream, full) in enumerate(CALLS):
                    if cl != l:
                        continue
                    act.wait_ge(s_modc, l + 1)
                    for t in range(NT):
                        act.wait_ge(t_utp.sem, t_utp.at(m, t + 1))
                        for k in range(KD):
                            last = a_(uT[:, k, t * P:(t + 1) * P], psum[:, 3 + 2 * t + k // 4, (k % 4) * P:(k % 4 + 1) * P],
                                      ACT.Identity, scale=modc[:, 8 + k, stream:stream + 1], bias=modc[:, k, stream:stream + 1])
                        last.then_inc(t_uT.sem, 1)

                    def product(kind, j):
                        s_ = (m, kind, j)
                        act.wait_ge(s_slab, SLAB_NO[s_] + 1)
                        return bank[BANK_NO[s_] % 2]

                    def conv_silu(j):
                        act.wait_ge(t_cv.sem, t_cv.at(m, j + 1))
                        if j < 6 and j >= 2:
                            act.wait_ge(t_ctp.sem, t_ctp.at(m, j - 1))
                        for a in range(2):
                            ch = 2 * j + a
                            if ch < XT_TILES:
                                dst = cxt[:, ch % 4, :]
                            elif ch < XT_TILES + GROUPS:
                                dst = bT[:, ch - XT_TILES, :]
                            else:
                                dst = cT[:, ch - XT_TILES - GROUPS, :]
                            last = a_(dst, cacc[:, ch % 4, :], ACT.Silu)
                        last.then_inc(t_cs.sem, 1)

                    def conv_out(j):
                        act.wait_ge(t_ctp.sem, t_ctp.at(m, j + 1))
                        src = bank[2 + 5 * (j % 2)].rearrange("p (c n) -> p c n", c=NT)
                        dst = xs[:, :, j * SW:(j + 1) * SW] if j < 6 else btok[:, :, (j - 6) * SW:(j - 5) * SW]
                        a_(dst, src, ACT.Copy).then_inc(t_xs.sem, 1)

                    if full:
                        for j in range(4):
                            src = product("four", j)
                            a_(fT[:, 2 * j:2 * j + 2, :], src.rearrange("p (a t) -> p a t", a=2), ACT.Copy).then_inc(s_read["act"], 1)
                    act.wait_ge(t_dtr.sem, t_dtr.at(m, 1))
                    a_(sp[1], sp[0], ACT.Exp, scale=-1.0).then_inc(t_dtx.sem, 1)
                    nx = 10 if full else 8
                    for j in range(nx):
                        src = product("xbc", j)
                        if j >= 2:
                            act.wait_ge(t_cs.sem, t_cs.at(m, j - 1))
                        for a in range(2):
                            ch = 2 * j + a
                            last = a_(cacc[:, ch % 4, :], src[:, a * SEQ:(a + 1) * SEQ], ACT.Identity,
                                      scale=par[:, 60 + 2 * 20 + ch:61 + 2 * 20 + ch], bias=par[:, 160 + ch:161 + ch])
                        last.then_inc(t_acc.sem, 1)
                        if j >= 1:
                            conv_silu(j - 1)
                        if 3 <= j:
                            conv_out(j - 3)
                    conv_silu(nx - 1)
                    conv_out(nx - 3) if nx == 10 else conv_out(5)
                    if nx == 8:
                        conv_out(6)
                        conv_out(7)
                    act.wait_ge(t_acu.sem, t_acu.at(m, 1))
                    a_(eac[:, :, :], acu[:, :, 0:48], ACT.Exp)
                    a_(ecd[:, :, :], acu[:, :, 48:96], ACT.Exp)
                    a_(sp[3], sp[2], ACT.Exp).then_inc(t_eac.sem, 1)
                    if full:
                        for j in range(6):
                            src = product("z", j)
                            a_(zs[:, :, j * SW:(j + 1) * SW], src.rearrange("p (c n) -> p c n", c=NT), ACT.Silu).then_inc(s_read["act"], 1)
                        for g in range(GROUPS + 1):
                            if g < GROUPS:
                                act.wait_ge(t_f1.sem, t_f1.at(m, g + 1))
                                if g >= 2:
                                    act.wait_ge(t_f2.sem, t_f2.at(m, g - 1))
                                a_(fA[:, g % 2, :, :], psum[:, 3:5, :], ACT.Copy).then_inc(t_f1c.sem, 1)
                            if g:
                                act.wait_ge(t_f2.sem, t_f2.at(m, g))
                                a_(fO[:, 2 * g - 2:2 * g, :], bank[6].rearrange("p (a t) -> p a t", a=2), ACT.Copy).then_inc(t_f2c.sem, 1)
                        for it in range(8):
                            act.wait_ge(t_seg.sem, t_seg.at(m, it + 1))
                            a_(seg[:, :, :, :], seg[:, :, :, :], ACT.Exp).then_inc(t_exp.sem, 1)
                            if it % 2 == 0:
                                j = it // 2
                                src = product("g2", j)
                                a_(gT[:, 2 * j:2 * j + 2, :], src.rearrange("p (a t) -> p a t", a=2), ACT.Sigmoid).then_inc(s_read["act"], 1)
                        for c in range(NT):
                            act.wait_ge(t_h.sem, t_h.at(m, c + 1))
                            act.wait_ge(t_y.sem, t_y.at(m, 8))
                            if c:
                                act.wait_ge(t_ss.sem, t_ss.at(m, c))
                            a_(seg[:, :, :, :].rearrange("p d h l -> p (d h l)"), zs[:, c, :], ACT.Square,
                               accum_out=rss[:, c, 0:1]).then_inc(t_ss.sem, 1)
                        for j in range(4):
                            src = product("g1", j)
                            act.wait_ge(t_mT2.sem, t_mT2.at(m, 4))
                            a_(gT[:, 2 * j:2 * j + 2, :], src.rearrange("p (a t) -> p a t", a=2), ACT.Sigmoid).then_inc(s_read["act"], 1)
                        for c in range(NT):
                            for b in range(3):
                                k = 3 * c + b
                                act.wait_ge(t_ytp.sem, t_ytp.at(m, k + 1))
                                for a in range(4):
                                    ch = 4 * b + a
                                    last = a_(ynT[:, ch, c * P:(c + 1) * P], bank[2 + 5 * (k % 2)][:, a * P:(a + 1) * P], ACT.Copy,
                                              scale=par[:, 48 + ch:49 + ch])
                                last.then_inc(t_yT.sem, 1)
                        act.wait_ge(t_gp.sem, t_gp.at(m, 1))
                        a_(grow[:, 0, :], psum[:, 3:5, :].rearrange("p b n -> p (b n)"), ACT.Copy).then_inc(t_gr.sem, 1)
                z, nt = e[l], len(MOE_TILES[l])
                def u2_copies(i):
                    v = MOE_TILES[l][i] // 2
                    act.wait_ge(s["u2_transposed"], of(l, "u2_transposed", i + 1))
                    for k in range(KD):
                        last = a_(u2T[:, k, i * P:(i + 1) * P], psum[:, 3 + k // 4, (k % 4) * P:(k % 4 + 1) * P],
                                  ACT.Identity, scale=modc[:, 32 + k, v:v + 1], bias=modc[:, 24 + k, v:v + 1])
                    last.then_inc(s["u2_ready"], 1)
                    act.wait_ge(s["logits"], of(l, "logits", i + 1))
                    if i >= 2:
                        act.wait_ge(s["routed"], of(l, "routed", i - 1))
                    a_(scores[i % 2], bank[2][:, 0:NE], ACT.Sigmoid).then_inc(s["scores"], 1)
                    act.wait_ge(s["back_tp"], of(l, "back_tp", i + 1))
                    a_(macc[:, i, :], psum[:, 5:7, :].rearrange("p b n -> p (b n)"), ACT.Copy).then_inc(s["back_copied"], 1)

                u2_copies(0)
                for i in range(nt):
                    act.wait_ge(s["shared_up"], of(l, "shared_up", i + 1))
                    if i >= 2:
                        act.wait_ge(s["shared_h"], of(l, "shared_h", i - 1))
                    a_(hs[i % 2], bank[i % 2][:, 0:FF], ACT.Silu).then_inc(s["shared_sil"], 1)
                    if i + 1 < nt:
                        u2_copies(i + 1)
                    act.wait_ge(s["shared_y"], of(l, "shared_y", i + 1))
                    act.wait_ge(s[f"u2_stored{i % 2}"], of(l, f"u2_stored{i % 2}", 16 * (i // 2 + 1)))
                    a_(macc[:, i, :], psum[:, 5:7, :].rearrange("p b n -> p (b n)"), ACT.Copy).then_inc(s["shared_out"], 1)
                for v in range(nt // 2):
                    for k in range(KD):
                        a_(ln2x[:, v, k * P:(k + 1) * P], ident, ACT.Copy, scale=modc[:, 40 + k, v:v + 1]).then_inc(s["g2_diag"], 1)
                    act.wait_ge(s["g2_rows"], of(l, "g2_rows", v + 1))
                    a_(grow[:, v, :], psum[:, 2:4, :].rearrange("p b n -> p (b n)"), ACT.Copy).then_inc(s["g2_ready"], 1)
                act.wait_ge(s["g2_ready"], of(l, "g2_ready", nt // 2))
                act.sem_inc(z["xt_act"], 1)
                act.sem_inc(z["y_act"], 1)
                act.wait_ge(s["blocks_ready"], of(l, "blocks_ready", 1))
                n = act.value_load(bexp[0:1, P:P + 1], min_val=1, max_val=NB)

                def x_copy(i, b2):
                    act.wait_ge(z["xt_tp"], i + 4)
                    act.wait_ge(z["up"], i + 1)
                    a_(xTe[b2][:, 0:4, :], bank[2].rearrange("p (k t) -> p k t", k=4), ACT.Copy).then_inc(z["xt_act"], 1)

                x_copy(0, 0)
                x_copy(1, 1)
                with act.Fori(0, NB // UNR) as ii:
                    with act.If(n > ii * UNR):
                        for u in range(UNR):
                            i = ii * UNR + u
                            with act.If(n > i):
                                act.wait_ge(z["up"], i + 3)
                                act.wait_ge(z["h_ready"], i + 1)
                                a_(hs[u % 2], bank[u % 2][:, 0:FF], ACT.Silu).then_inc(z["silu"], 1)
                            with act.If(n > i + 2):
                                x_copy(i + 2, u % 2)
                            with act.If(n > i):
                                act.wait_ge(z["down"], i + 4)
                                act.wait_ge(e_s[l][u % 2], 16 * (ii * 3 + u // 2 + 1))
                                a_(ysb[u % 2][:, 0:512], bank[5], ACT.Copy).then_inc(z["y_act"], 1)

        @block.vector
        def _(dve):
            V = nc.vector
            count = {"chain": 0, "ln": 0}

            def link(ins_):
                count["chain"] += 1
                ins_.then_inc(s_chain, 1)
                dve.wait_ge(s_chain, count["chain"])

            def inverse_root(v, scale):
                link(V.tensor_scalar(rsq[:, 0:1], v, scale, EPS, ALU.mult, ALU.add))
                link(V.tensor_scalar(rsqi[:, 0:1], rsq[:, 0:1].bitcast(I32), 1, None, ALU.logical_shift_right))
                link(V.tensor_scalar(rsqi[:, 1:2], rsqi[:, 0:1], -1.0, float(0x5f3759df), ALU.mult, ALU.add))
                link(V.tensor_scalar(rsq[:, 1:2], rsq[:, 0:1], -0.5, None, ALU.mult))
                y = rsqi[:, 1:2].bitcast(F32)
                for _ in range(3):
                    link(V.scalar_tensor_tensor(rsq[:, 2:3], y, rsq[:, 1:2], y, ALU.mult, ALU.mult))
                    link(V.scalar_tensor_tensor(rsq[:, 3:4], rsq[:, 2:3], 1.5, y, ALU.add, ALU.mult))
                    y = rsq[:, 3:4]

            def norm(dst, src, last=None):
                for hlf in range(2):
                    i_ = V.bn_stats(stat[:, hlf, :], src[:, hlf * 512:(hlf + 1) * 512])
                link(i_)
                link(V.bn_aggr(mv[:, :], stat[:, :, :].rearrange("p a b -> p (a b)")))
                inverse_root(mv[:, 1:2], 1.0)
                i_ = V.tensor_scalar(dst, src, mv[:, 0:1], rsq[:, 3:4], ALU.subtract, ALU.mult)
                if last is None:
                    link(i_)
                else:
                    i_.then_inc(last, 1)

            def post_norm(t, tmp, which):
                norm(tmp, tmp)
                dve.wait_ge(s_lnrow, 32 * (which + 1))
                link(V.tensor_tensor(tmp, tmp, lnrow[:, 0, :], ALU.mult))
                return V.tensor_tensor(xres[:, t, :], tmp, lnrow[:, 1, :], ALU.add)

            dve.wait_ge(s_const, 16)
            dve.wait_ge(s_x, 16 * 8)
            for t in range(NT):
                link(V.tensor_tensor(xres[:, t, :], xres[:, t, :], ring[0].rearrange("p k n -> p (k n)")[:, t * D:(t + 1) * D], ALU.add))
            dve.sem_inc(s_xin, 1)
            which = 0
            for l in range(DEPTH):
                dve.wait_ge(s_parc, 2 * l + 2)
                dve.wait_ge(s_ada_tp, l + 1)
                link(V.tensor_tensor(modc[:, :, :], bank[3][:, 0:96].rearrange("p (j v) -> p j v", v=2),
                                     par[:, 0:48].unsqueeze(2).to_broadcast([P, 48, 2]), ALU.add))
                link(V.tensor_scalar(modc[:, 8:16, :], modc[:, 8:16, :], 1.0, None, ALU.add))
                V.tensor_scalar(modc[:, 32:40, :], modc[:, 32:40, :], 1.0, None, ALU.add).then_inc(s_modc, 1)
                dve.wait_ge(s_modc, l + 1)

                def u2_norm(i):
                    if i >= 2:
                        dve.wait_ge(s["u2_transposed"], of(l, "u2_transposed", i - 1))
                    norm(ln2x[:, i % 2, :], xres[:, MOE_TILES[l][i], :], s["u2_normed"])

                for m, (cl, stream, full) in enumerate(CALLS):
                    if cl != l:
                        continue
                    if not (m and CALLS[m - 1][0] == l and CALLS[m - 1][2]):
                        for t in range(NT):
                            norm(lnx[:, t, :], xres[:, TILES[stream][t], :], t_lnx.sem)

                    def product(kind, j):
                        s_ = (m, kind, j)
                        dve.wait_ge(s_slab, SLAB_NO[s_] + 1)
                        return bank[BANK_NO[s_] % 2]

                    src = product("dt", 0).rearrange("p (c n) -> p c n", c=NT)[:, :, 0:48]
                    bias = hpar[:, 0:48].unsqueeze(1).to_broadcast([P, NT, 48])
                    V.tensor_tensor(sp[2], src, bias, ALU.add).then_inc(s_read["dve"], 1)
                    dve.wait_ge(s_read["dve"], freed(BANK_NO[(m, "dt", 0)])[1])
                    link(V.tensor_scalar(sp[3], sp[2], -1.0, None, ALU.mult))
                    V.tensor_tensor(sp[0], sp[2], sp[3], ALU.max).then_inc(t_dtr.sem, 1)
                    dve.wait_ge(t_dtx.sem, t_dtx.at(m, 1))
                    link(V.tensor_scalar(sp[3], sp[1], 2.0, None, ALU.add))
                    link(V.reciprocal(sp[3], sp[3]))
                    link(V.tensor_tensor(sp[1], sp[1], sp[3], ALU.mult))
                    link(V.tensor_tensor(sp[3], sp[1], sp[1], ALU.mult))
                    link(V.tensor_scalar(sp[0], sp[3], 2.0 / 17, 2.0 / 15, ALU.mult, ALU.add))
                    for d_ in (13, 11, 9, 7, 5, 3, 1):
                        link(V.tensor_tensor(sp[0], sp[0], sp[3], ALU.mult))
                        link(V.tensor_scalar(sp[0], sp[0], 2.0 / d_, None, ALU.add))
                    link(V.tensor_tensor(sp[0], sp[0], sp[1], ALU.mult))
                    link(V.tensor_scalar(sp[2], sp[2], 0.0, None, ALU.max))
                    link(V.tensor_tensor(dtv[:, :, :], sp[0], sp[2], ALU.add))
                    V.tensor_tensor(adt[:, :, :], dtv[:, :, :], aneg[:, :].unsqueeze(1).to_broadcast([P, NT, 48]), ALU.mult).then_inc(t_adt.sem, 1)

                    for j in range(10 if full else 8):
                        src = product("xbc", j)
                        dve.wait_ge(t_acc.sem, t_acc.at(m, j + 1))
                        for tap in (0, 1, 3, 4):
                            sh = tap - CONVW // 2
                            lo, hi = max(0, -sh), min(SEQ, SEQ - sh)
                            for a in range(2):
                                ch = 2 * j + a
                                dst = cacc[:, ch % 4, lo:hi]
                                i_ = V.scalar_tensor_tensor(dst, src[:, a * SEQ + lo + sh:a * SEQ + hi + sh],
                                                            par[:, 60 + tap * 20 + ch:61 + tap * 20 + ch], dst, ALU.mult, ALU.add)
                                if tap == 4 and a == 1:
                                    i_.then_inc(t_cv.sem, 1)
                                    dve.wait_ge(t_cv.sem, t_cv.at(m, j + 1))
                                elif a == 1 or tap == 4:
                                    link(i_)
                        dve.sem_inc(s_read["dve"], 1)

                    dve.wait_ge(t_acp.sem, t_acp.at(m, 1))
                    link(V.tensor_copy(acu[:, :, :], bank[5][:, 0:NT * 96].rearrange("p (c n) -> p c n", c=NT)))
                    V.tensor_tensor(sp[2], acu[:, :, 48:96], acu[:, :, 0:48], ALU.subtract).then_inc(t_acu.sem, 1)
                    dve.wait_ge(t_eac.sem, t_eac.at(m, 1))
                    V.tensor_tensor(dec[:, :, :], sp[3], dtv[:, :, :], ALU.mult).then_inc(t_dec.sem, 1)
                    dve.wait_ge(t_xs.sem, t_xs.at(m, 6))
                    dve.wait_ge(t_dec.sem, t_dec.at(m, 1))

                    def state_round(i, d, c, g, dst, prev):
                        if i >= 2:
                            dve.wait_ge(t_stp.sem, t_stp.at(m, i - 1))
                        h0 = d * HEADS + g * HPG
                        V.tensor_tensor(wst[:, i % 2, :].rearrange("p (h d) -> p h d", h=HPG),
                                        xs[:, c, g * GW:(g + 1) * GW].rearrange("p (h d) -> p h d", h=HPG),
                                        dec[:, c, h0:h0 + HPG].unsqueeze(2).to_broadcast([P, HPG, HD]), ALU.mult).then_inc(t_w.sem, 1)

                    def state_add(i, d, c, g, dst, prev):
                        dve.wait_ge(t_stp.sem, t_stp.at(m, i + 1))
                        h0 = d * HEADS + g * HPG
                        src = bank[5 + i % 2][:, 0:GW].rearrange("p (h d) -> p h d", h=HPG)
                        hsl = slice(g * HPG, (g + 1) * HPG)
                        if prev is None:
                            V.tensor_copy(dst[:, hsl, :], src).then_inc(t_st.sem, 1)
                        else:
                            link(V.tensor_tensor(dst[:, hsl, :], prev[:, hsl, :],
                                                 ecd[:, c, h0:h0 + HPG].unsqueeze(2).to_broadcast([P, HPG, HD]), ALU.mult))
                            V.tensor_tensor(dst[:, hsl, :], dst[:, hsl, :], src, ALU.add).then_inc(t_st.sem, 1)

                    def state_pass(lst, base):
                        for i, a_ in enumerate(lst):
                            state_round(base + i, *a_)
                            if i:
                                state_add(base + i - 1, *lst[i - 1])
                        state_add(base + len(lst) - 1, *lst[-1])

                    init = stream == 1
                    state_pass([(0, 0, g, st[0][1], None if init else st[0][0]) for g in range(4)]
                               + [(1, 1, g, st[1][1], None if init else st[1][0]) for g in range(4)], 0)

                    if full:
                        dsk = hpar[:, 96:120]

                        def head(it):
                            c, g = it // GROUPS, it % GROUPS
                            if it:
                                dve.wait_ge(t_y.sem, t_y.at(m, it))
                            for d in range(2):
                                dve.wait_ge(t_row.sem, t_row.at(m, 2 * it + d + 1))
                                h0 = d * HEADS + g * HPG
                                src = psum[:, 3:5, :].rearrange("p b n -> p (b n)")
                                V.tensor_tensor(seg[:, d, :, :], src[:, 0:768].rearrange("p (h l) -> p h l", h=HPG),
                                                acu[:, c, h0:h0 + HPG].unsqueeze(2).to_broadcast([P, HPG, P]), ALU.subtract).then_inc(t_rowr.sem, 1)
                            dve.wait_ge(t_rowr.sem, t_rowr.at(m, 2 * it + 2))
                            V.tensor_scalar(seg[:, :, :, :], seg[:, :, :, :], 0.0, None, ALU.min).then_inc(t_seg.sem, 1)
                            link(V.tensor_tensor(smask[:, 0, :], src[:, 768:896], tri_le, ALU.mult))
                            V.tensor_tensor(smask[:, 1, :], src[:, 768:896], tri_ge, ALU.mult).then_inc(t_sm.sem, 1)

                        def weigh(it):
                            dve.wait_ge(t_exp.sem, t_exp.at(m, it + 1))
                            dve.wait_ge(t_sm.sem, t_sm.at(m, it + 1))
                            V.tensor_tensor(seg[:, 0, :, :], seg[:, 0, :, :], smask[:, 0, :].unsqueeze(1).to_broadcast([P, HPG, P]), ALU.mult).then_inc(t_lmF.sem, 1)

                        def merge_four(j):
                            src = product("bf", j)
                            dve.wait_ge(s_read["act"], freed(BANK_NO[(m, "g2", j)])[1])
                            V.tensor_tensor(mT[:, 2 * j:2 * j + 2, :], gT[:, 2 * j:2 * j + 2, :], src.rearrange("p (a t) -> p a t", a=2), ALU.mult).then_inc(s_read["dve"], 1)
                            dve.wait_ge(s_read["dve"], freed(BANK_NO[(m, "bf", j)])[1])
                            dve.sem_inc(t_mT2.sem, 1)

                        def tail(it):
                            c, g = it // GROUPS, it % GROUPS
                            dve.wait_ge(t_y.sem, t_y.at(m, it + 1))
                            xv = xs[:, c, g * GW:(g + 1) * GW].rearrange("p (h d) -> p h d", h=HPG)
                            v3 = lambda a: a.rearrange("p (h d) -> p h d", h=HPG)
                            hb = lambda a: a.unsqueeze(2).to_broadcast([P, HPG, HD])
                            y0, y1, y2 = (ytmp[:, b, :] for b in range(3))
                            link(V.tensor_tensor(v3(y0), xv, hb(dsk[:, g * HPG:(g + 1) * HPG]), ALU.mult))
                            link(V.tensor_tensor(y0, y0, bank[5][:, 0:GW], ALU.add))
                            for d in range(2):
                                w_ = c if d == 0 else 1 - c
                                if stream == 0 or w_ == 1:
                                    h0 = d * HEADS + g * HPG
                                    link(V.tensor_tensor(v3(y1), v3(bank[6 + d][:, 0:GW]), hb(eac[:, c, h0:h0 + HPG]), ALU.mult))
                                    link(V.tensor_tensor(y0, y0, y1, ALU.add))
                            dve.sem_inc(t_yr.sem, 1)
                            zz = zs[:, c, g * GW:(g + 1) * GW]
                            dve.wait_ge(s_read["act"], freed(BANK_NO[(m, "z", 5)])[1])
                            i_ = V.tensor_tensor(zz, y0, zz, ALU.mult)
                            if g == GROUPS - 1:
                                i_.then_inc(t_h.sem, 1)

                        for it in range(8):
                            head(it)
                            if it:
                                tail(it - 1)
                            weigh(it)
                            if it % 2 == 0 and it:
                                merge_four(it // 2 - 1)
                        merge_four(3)
                        tail(7)

                    if stream == 1:
                        if full:
                            dve.wait_ge(t_y.sem, t_y.at(m, 8))
                        state_pass([(0, 1, g, st[0][0], st[0][1]) for g in range(4)]
                                   + [(1, 0, g, st[1][0], st[1][1]) for g in range(4)], 8)

                    if full:
                        dve.wait_ge(t_h.sem, t_h.at(m, 2))
                        for c in range(NT):
                            dve.wait_ge(t_ss.sem, t_ss.at(m, c + 1))
                            inverse_root(rss[:, c, 0:1], 1.0 / DIN)
                            V.tensor_scalar(zs[:, c, :], zs[:, c, :], rsq[:, 3:4], None, ALU.mult).then_inc(t_yn.sem, 1)
                        for k in range(KD):
                            V.tensor_scalar(lnx[:, 0, k * P:(k + 1) * P], ident, modc[:, 16 + k, stream:stream + 1], None, ALU.mult).then_inc(t_gd.sem, 1)
                        for j in range(4):
                            dve.wait_ge(s_slab, SLAB_NO[(m, "bsb", j)] + 1)
                            dve.wait_ge(s_read["act"], freed(BANK_NO[(m, "g1", j)])[1])
                            src = bank[BANK_NO[(m, "bsb", j)] % 2].rearrange("p (a t) -> p a t", a=2)
                            g_ = gT[:, 2 * j:2 * j + 2, :]
                            V.tensor_tensor(g_, g_, src, ALU.mult).then_inc(s_read["dve"], 1)
                            dve.wait_ge(s_read["dve"], freed(BANK_NO[(m, "bsb", j)])[1])
                            V.tensor_tensor(mT[:, 2 * j:2 * j + 2, :], mT[:, 2 * j:2 * j + 2, :], g_, ALU.add).then_inc(t_mT.sem, 1)
                        dve.wait_ge(t_gr.sem, t_gr.at(m, 1))
                        if CALLS[m + 1:m + 2] and CALLS[m + 1][0] == l:
                            for t in range(NT):
                                norm(lnx[:, t, :], xres[:, TILES[CALLS[m + 1][1]][t], :], t_lnx.sem)
                        early = [i for i in range(2) if MOE_TILES[l][i] not in TILES[stream]]
                        if stream == 0:
                            for i in early:
                                u2_norm(i)
                        for j in range(4):
                            src = product("wo", j).rearrange("p (c n) -> p c n", c=NT)
                            V.tensor_tensor(yrow[:, :, :], src, grow[:, 0, j * SW:(j + 1) * SW].unsqueeze(1).to_broadcast([P, NT, SW]), ALU.mult).then_inc(s_read["dve"], 1)
                            dve.wait_ge(s_read["dve"], freed(BANK_NO[(m, "wo", j)])[1])
                            t0 = TILES[stream][0]
                            xv = xres[:, t0:t0 + NT, j * SW:(j + 1) * SW]
                            link(V.scalar_tensor_tensor(xv, xv, ALPHA, yrow[:, :, :], ALU.mult, ALU.add))
                        for t in range(NT):
                            i_ = post_norm(TILES[stream][t], xres[:, TILES[stream][t], :], which)
                            if t == NT - 1:
                                i_.then_inc(s_lnrow_free, 1)
                                dve.wait_ge(s_lnrow_free, which + 1)
                            else:
                                link(i_)
                            if stream == 0 and t not in early:
                                u2_norm(t)
                        which += 1

                z, nt = e[l], len(MOE_TILES[l])
                big = 3.0e38
                _, sel, s3, mk, cum, pos, pend, base = rt

                for i in range(nt):
                    sc = scores[i % 2]
                    dve.wait_ge(s["scores"], of(l, "scores", i + 1))
                    dve.wait_ge(s["router_in"], of(l, "router_in", 32))
                    link(V.tensor_tensor(sel, sc, rbias, ALU.add))
                    g3 = sel.rearrange("p (g e) -> p g e", g=NGRP)
                    for g in range(NGRP):
                        link(V.max(r8[1], sel[:, g * EPG:(g + 1) * EPG]))
                        link(V.tensor_tensor(r8[2][:, g:g + 1], r8[1][:, 0:1], r8[1][:, 1:2], ALU.add))
                    sq = lambda v_: v_.rearrange("p (g e) -> p g e", g=NGRP)
                    other = r8[2].unsqueeze(1).to_broadcast([P, NGRP, NGRP])
                    own = r8[2].unsqueeze(2).to_broadcast([P, NGRP, NGRP])
                    link(V.tensor_tensor(sq(mk), other, own, ALU.is_equal))
                    link(V.tensor_tensor(mk, mk, cst[:, C_TRI8:C_TRI8 + NGRP * NGRP], ALU.mult))
                    link(V.tensor_tensor(sq(cum), other, own, ALU.is_gt))
                    link(V.tensor_tensor(mk, mk, cum, ALU.add))
                    link(V.tensor_reduce(r8[1], sq(mk), AX.X, ALU.add))
                    link(V.tensor_scalar(r8[3], r8[1], float(TOPG), None, ALU.is_lt))
                    link(V.tensor_scalar(r8[0], r8[3], big, -big, ALU.mult, ALU.add))
                    gsel = r8[3].unsqueeze(2).to_broadcast([P, NGRP, EPG])
                    gneg = r8[0].unsqueeze(2).to_broadcast([P, NGRP, EPG])
                    link(V.tensor_tensor(s3.rearrange("p (g e) -> p g e", g=NGRP), g3, gsel, ALU.mult))
                    link(V.tensor_tensor(s3.rearrange("p (g e) -> p g e", g=NGRP), s3.rearrange("p (g e) -> p g e", g=NGRP), gneg, ALU.add))
                    link(V.max(r8[1], s3))
                    link(V.match_replace(mk, r8[1], s3, big))
                    link(V.tensor_scalar(msk[:, i, :], mk, big, None, ALU.is_equal))
                    link(V.tensor_tensor_scan(cum, ones[:, 0:NE], msk[:, i, :], 0.0, ALU.mult, ALU.add))
                    link(V.tensor_tensor(cum, cum, msk[:, i, :], ALU.mult))
                    link(V.tensor_scalar(cum, cum, -1.0, None, ALU.add))
                    c3 = cube.rearrange("p (j e) -> p j e", j=TOPK)
                    link(V.tensor_tensor(c3, cst[:, C_RANK:C_RANK + TOPK * NE].rearrange("p (j e) -> p j e", j=TOPK),
                                         cum.unsqueeze(1).to_broadcast([P, TOPK, NE]), ALU.is_equal))
                    link(V.tensor_tensor(c3, c3, sc.unsqueeze(1).to_broadcast([P, TOPK, NE]), ALU.mult))
                    link(V.tensor_reduce(gat[:, i, :], c3, AX.X, ALU.add))
                    link(V.tensor_reduce(r8[0][:, 0:1], gat[:, i, :], AX.X, ALU.add))
                    link(V.reciprocal(r8[0][:, 0:1], r8[0][:, 0:1]))
                    V.tensor_scalar(gat[:, i, :], gat[:, i, :], r8[0][:, 0:1], 2.5, ALU.mult, ALU.mult).then_inc(s["routed"], 1)
                    dve.wait_ge(s["routed"], of(l, "routed", i + 1))
                    dve.wait_ge(s["shared_sil"], of(l, "shared_sil", i + 1))
                    V.tensor_tensor(hh[i % 2], hs[i % 2], bank[i % 2][:, FF:2 * FF], ALU.mult).then_inc(s["shared_h"], 1)
                    if i + 2 < nt:
                        u2_norm(i + 2)
                    dve.wait_ge(s["shared_ht"], of(l, "shared_ht", i + 1))
                    V.tensor_copy(hT[i % 2], bank[4][:, 0:2 * P].rearrange("p (k t) -> p k t", k=2)).then_inc(s["shared_htc"], 1)
                dve.wait_ge(s["counted"], of(l, "counted", 1))
                cnt = bank[7][:, 4 * NE:5 * NE]
                link(V.tensor_scalar(mk, cnt, 0.0, None, ALU.is_gt))
                for k in range(1, nt):
                    link(V.scalar_tensor_tensor(mk, cnt, float(k * P), mk, ALU.is_gt, ALU.add))
                link(V.tensor_tensor_scan(pend, ones[:, 0:NE], mk, 0.0, ALU.mult, ALU.add))
                link(V.tensor_tensor(base, pend, mk, ALU.subtract))
                for i in range(nt):
                    ps = bank[7][:, i * NE:(i + 1) * NE]
                    link(V.tensor_scalar(s3, ps, float(P), None, ALU.is_ge))
                    for k in range(2, nt):
                        link(V.scalar_tensor_tensor(s3, ps, float(k * P), s3, ALU.is_ge, ALU.add))
                    link(V.scalar_tensor_tensor(pos, s3, -float(P), ps, ALU.mult, ALU.add))
                    link(V.scalar_tensor_tensor(pos, pos, float(NB), s3, ALU.mult, ALU.add))
                    link(V.tensor_tensor(pos, pos, base, ALU.add))
                    link(V.tensor_tensor_scan(cum, ones[:, 0:NE], msk[:, i, :], 0.0, ALU.mult, ALU.add))
                    link(V.tensor_tensor(cum, cum, msk[:, i, :], ALU.mult))
                    link(V.tensor_scalar(cum, cum, -1.0, None, ALU.add))
                    c3 = cube.rearrange("p (j e) -> p j e", j=TOPK)
                    link(V.tensor_tensor(c3, cst[:, C_RANK:C_RANK + TOPK * NE].rearrange("p (j e) -> p j e", j=TOPK),
                                         cum.unsqueeze(1).to_broadcast([P, TOPK, NE]), ALU.is_equal))
                    link(V.tensor_tensor(c3, c3, pos.unsqueeze(1).to_broadcast([P, TOPK, NE]), ALU.mult))
                    link(V.tensor_reduce(slotf[:, i, :], c3, AX.X, ALU.add))
                    link(V.tensor_copy(sloti[:, i, :], slotf[:, i, :]))
                    link(V.tensor_scalar(slotf[:, i, :], cst[:, C_TOK:C_TOK + TOPK], float(i * P * TOPK), None, ALU.add))
                    V.tensor_copy(tokid[:, i, :], slotf[:, i, :]).then_inc(s["table_ready"], 1)
                    dve.wait_ge(s["table_ready"], of(l, "table_ready", i + 1))
                link(V.tensor_scalar(s3, pend, cst[:, C_P:C_P + 1], None, ALU.is_le))
                link(V.tensor_reduce(ecol[:, :], s3, AX.X, ALU.add))
                V.tensor_scalar(ecol[:, :], ecol[:, :], float(NE - 1), None, ALU.min).then_inc(s["placed"], 1)
                link(V.tensor_copy(bexp[0:1, P:P + 1], pend[0:1, NE - 1:NE]))
                dve.wait_ge(s["rank_tp"], of(l, "rank_tp", 1))
                V.tensor_copy(bexp[0:1, 0:P], bank[7][0:1, 0:P]).then_inc(s["blocks_ready"], 1)
                dve.wait_ge(s["blocks_ready"], of(l, "blocks_ready", 1))
                dve.wait_ge(s["table_in"], of(l, "table_in", 16))
                V.tensor_scalar(tblg[:, 0:NB], tbl[:, 0:NB], 3, None, ALU.logical_shift_right).then_inc(s_shift[l], 1)
                dve.sem_inc(z["xt_dve"], 1)
                dve.sem_inc(z["y_dve"], 1)
                dve.sem_inc(z["h_ready"], 2)
                dve.sem_inc(z["ht_copied"], 1)
                n = dve.value_load(bexp[0:1, P:P + 1], min_val=1, max_val=NB)

                def x_copy(i, b2):
                    dve.wait_ge(z["xt_tp"], i + 4)
                    dve.wait_ge(z["up"], i + 1)
                    V.tensor_copy(xTe[b2][:, 4:8, :], bank[3].rearrange("p (k t) -> p k t", k=4)).then_inc(z["xt_dve"], 1)

                x_copy(0, 0)
                x_copy(1, 1)
                with dve.Fori(0, NB // UNR) as ii:
                    with dve.If(n > ii * UNR):
                        for u in range(UNR):
                            i = ii * UNR + u
                            with dve.If(n > i):
                                dve.wait_ge(z["silu"], i + 1)
                                dve.wait_ge(z["ht_tp"], i + 1)
                                V.tensor_tensor(hh[u % 2], hs[u % 2], bank[u % 2][:, FF:2 * FF], ALU.mult).then_inc(z["h_ready"], 1)
                            with dve.If(n > i + 2):
                                x_copy(i + 2, u % 2)
                            with dve.If(n > i):
                                dve.wait_ge(z["ht_tp"], i + 3)
                                dve.wait_ge(z["down"], i + 2)
                                V.tensor_copy(hT[u % 2], bank[4][:, 0:2 * P].rearrange("p (k t) -> p k t", k=2)).then_inc(z["ht_copied"], 1)
                                dve.wait_ge(z["down"], i + 4)
                                dve.wait_ge(e_s[l][u % 2], 16 * (ii * 3 + u // 2 + 1))
                                V.tensor_copy(ysb[u % 2][:, 512:1024], bank[6]).then_inc(z["y_dve"], 1)
                for i in range(nt):
                    t = MOE_TILES[l][i]
                    dve.wait_ge(s["shared_out"], of(l, "shared_out", i + 1))
                    for j in range(TOPK):
                        if j % 4 == 0:
                            dve.wait_ge(e_yin[j // 4], 16 * (i + 1 + (nt0 if l else 0)))
                        link(V.scalar_tensor_tensor(macc[:, i, :], yall[i % 2][:, j, :], gat[:, i, j:j + 1], macc[:, i, :], ALU.mult, ALU.add))
                    link(V.tensor_tensor(macc[:, i, :], macc[:, i, :], grow[:, t // 2, :], ALU.mult))
                    link(V.scalar_tensor_tensor(xres[:, t, :], xres[:, t, :], ALPHA, macc[:, i, :], ALU.mult, ALU.add))
                    i_ = post_norm(t, xres[:, t, :], which)
                    i_.then_inc(e_comb[l], 1)
                    dve.wait_ge(e_comb[l], i + 1)
                dve.sem_inc(s_lnrow_free, 1)
                which += 1

        @block.gpsimd
        def _(gp):
            G = nc.gpsimd
            count = {"chain": 0}

            def link(ins_):
                count["chain"] += 1
                ins_.then_inc(s_pchain, 1)
                gp.wait_ge(s_pchain, count["chain"])

            link(gp.memset(sent[:, :], SENTINEL))
            for l in range(DEPTH):
                z, nt = e[l], len(MOE_TILES[l])
                gp.dma_start(scratch["tbl"][l].rearrange("(p b) o -> p (b o)", b=NB), sent[:, :]).then_inc(s["sentinel_in"], 16)
                for m, (cl, stream, full) in enumerate(CALLS):
                    if cl != l or not full:
                        continue
                    gp.wait_ge(t_xs.sem, t_xs.at(m, 6))
                    gp.wait_ge(t_dec.sem, t_dec.at(m, 1))
                    for it in range(8):
                        c, g = it // GROUPS, it % GROUPS
                        if it >= 2:
                            gp.wait_ge(t_y.sem, t_y.at(m, it - 1))
                        for d in range(2):
                            h0 = d * HEADS + g * HPG
                            last = G.tensor_tensor(xdt[:, it % 2, d, :].rearrange("p (h d) -> p h d", h=HPG),
                                                   xs[:, c, g * GW:(g + 1) * GW].rearrange("p (h d) -> p h d", h=HPG),
                                                   dtv[:, c, h0:h0 + HPG].unsqueeze(2).to_broadcast([P, HPG, HD]), ALU.mult)
                        last.then_inc(t_xd.sem, 1)
                        gp.wait_ge(t_exp.sem, t_exp.at(m, it + 1))
                        gp.wait_ge(t_sm.sem, t_sm.at(m, it + 1))
                        G.tensor_tensor(seg[:, 1, :, :], seg[:, 1, :, :], smask[:, 1, :].unsqueeze(1).to_broadcast([P, HPG, P]), ALU.mult).then_inc(t_lmB.sem, 1)
                gp.wait_ge(s["routed"], of(l, "routed", 1))
                for b in range(3):
                    last = G.memset(xg[b], 0.0)
                link(last)
                gp.wait_ge(s["sentinel_in"], of(l, "sentinel_in", 16))
                for b in range(2):
                    gp.dma_start(first[:, b:b + 1], sent[:, b:b + 1]).then_inc(e_s[l][b], 16)
                for i in range(nt):
                    gp.wait_ge(s["table_ready"], of(l, "table_ready", i + 1))
                    for j in range(TOPK):
                        gp.indirect_dma_start(scratch["tbl"][l], bass.IndirectOffsetOnAxis(ap=sloti[:, i, j:j + 1], axis=0),
                                              tokid[:, i, j:j + 1], None, bounds_check=P * NB - 1, oob_is_err=False).then_inc(s["table_scattered"], 16)
                gp.wait_ge(s["table_scattered"], of(l, "table_scattered", 16 * nt * TOPK))
                gp.dma_start(tbl[:, 0:NB], scratch["tbl"][l].rearrange("(p b) o -> p (b o)", b=NB)).then_inc(s["table_in"], 16)
                gp.wait_ge(s["table_in"], of(l, "table_in", 16))
                gp.wait_ge(s["blocks_ready"], of(l, "blocks_ready", 1))
                for b in range(2):
                    gp.wait_ge(s[f"u2_stored{b}"], of(l, f"u2_stored{b}", 8 * nt))
                n = gp.value_load(bexp[0:1, P:P + 1], min_val=1, max_val=NB)
                gp.wait_ge(s_shift[l], 1)

                last_token = gp.to_reg(nt * P - 1)
                last_row = gp.to_reg(nt * P * TOPK - 1)

                def gather(i, b3, b6):
                    G.tensor_copy(idg[:, b6:b6 + 1], tblg[:, bass.ds(i, 1)]).then_inc(s_idg[l], 1)
                    gp.wait_ge(z["xt_tp"], i + 1)
                    gp.wait_ge(s_idg[l], i + 1)
                    gp.sem_inc(s_passed, 1)
                    gp.indirect_dma_start(xg[b3], None, scratch["u2"][l], bass.IndirectOffsetOnAxis(ap=idg[:, b6:b6 + 1], axis=0),
                                          bounds_check=last_token, oob_is_err=False).then_inc(e_g[l][b3], 16)

                for i in range(4):
                    gather(i, i % 3, i)
                with gp.Fori(0, NB // UNR) as ii:
                    with gp.If(n > ii * UNR):
                        for u in range(UNR):
                            i = ii * UNR + u
                            with gp.If(n > i + 4):
                                gather(i + 4, (u + 1) % 3, (u + 4) % UNR)
                            with gp.If(n > i):
                                G.tensor_copy(ids[:, u:u + 1], tbl[:, bass.ds(i, 1)]).then_inc(s_ids[l], 1)
                                gp.wait_ge(s_ids[l], i + 1)
                                gp.wait_ge(z["y_act"], i + 2)
                                gp.wait_ge(z["y_dve"], i + 2)
                                gp.sem_inc(s_passed, 1)
                                gp.indirect_dma_start(scratch["y"][l], bass.IndirectOffsetOnAxis(ap=ids[:, u:u + 1], axis=0),
                                                      ysb[u % 2], None, bounds_check=last_row, oob_is_err=False).then_inc(e_s[l][u % 2], 16)
                stored = [gp.snap(((n + 1) // 2 + 1) * 16), gp.snap((n // 2 + 1) * 16)]
                for b in range(2):
                    gp.wait_ge(e_s[l][b], stored[b])
                gp.sem_inc(e_done, 1)
                for i in range(nt):
                    if i >= 2:
                        gp.wait_ge(e_comb[l], i - 1)
                    if l + 1 < DEPTH:
                        gp.wait_ge(s_ada_mm, 4 + 28 * (l + 1) + 5 * i + 1)
                    for h, ranks in enumerate((slice(0, 4), slice(4, 8))):
                        if i or l:
                            gp.wait_ge(e_yin[h], 16 * (i + (nt0 if l else 0)))
                        gp.dma_start(yall[i % 2][:, ranks, :],
                                     scratch["y"][l][i * P * TOPK:(i + 1) * P * TOPK, :].rearrange("(p j) n -> p j n", j=TOPK)[:, ranks, :]).then_inc(e_yin[h], 16)


_INS = ["x", "c", "ctx", "c_ctx", "w_ada", "b_ada", "w_in", "conv_w", "conv_b", "dt_bias", "a_log", "d_skip",
        "ssm_norm_w", "w_br_ssm", "w_br_four", "w_out", "ln1_g", "ln1_b", "ln2_g", "ln2_b",
        "router_w", "router_bias", "w1", "w3", "w2", "ws1", "ws3", "ws2"]


def kernel(**inputs):
    import numpy as _np
    import concourse.bacc as _bacc
    from concourse import mybir as _mybir
    from concourse.bass_utils import run_bass_kernel_spmd as _run

    nc = _bacc.Bacc("TRN2", target_bir_lowering=False, num_devices=1)
    arrays, ins = {}, {}

    def dram(name, a):
        arrays[name] = a
        return nc.dram_tensor(name, a.shape, _mybir.dt.from_np(a.dtype), kind="ExternalInput").ap()

    for name in _INS:
        a = _np.ascontiguousarray(inputs[name])
        if name == "dt_bias" or name == "a_log":
            a = a.reshape(DEPTH, 2, HEADS)
        ins[name] = dram("in_" + name, a)
    pack, dfts, grid = host_constants()
    consts, dfts, grid = dram("const_pack", pack), dram("const_dft", dfts), dram("const_grid", grid)
    out = nc.dram_tensor("out_0", (1, SEQ, D), F32, kind="ExternalOutput").ap()
    scratch = {
        "u2": [nc.dram_tensor(f"tokens{l}", (len(MOE_TILES[l]) * P, D), F32, kind="Internal").ap() for l in range(DEPTH)],
        "y": [nc.dram_tensor(f"results{l}", (len(MOE_TILES[l]) * P * TOPK, D), F32, kind="Internal").ap() for l in range(DEPTH)],
        "tbl": [nc.dram_tensor(f"slots{l}", (P * NB, 1), I32, kind="Internal").ap() for l in range(DEPTH)],
    }
    hybrid_block_kernel(nc, ins, consts, dfts, grid, out, scratch)
    r = _run(nc, [arrays], core_ids=[0])
    return r.results[0]["out_0"]
```
